# Optimizing a Trainium2 kernel written in Bass

```python
import math
import jax, jax.numpy as jnp
from jax import lax
import numpy as np

D_MODEL = 1024
BATCH = 1
SEQ = 512
DEPTH = 2

CHUNK = 64
Q_BLOCK = 128
RMS_EPS = 1e-6
ROPE_BASE = 10000.0

RET_HEADS = 8
RET_QK_DIM = D_MODEL // RET_HEADS
RET_V_DIM = 2 * RET_QK_DIM
RET_QK_WIDTH = RET_HEADS * RET_QK_DIM
RET_WIDTH = RET_HEADS * RET_V_DIM
RET_IN = 2 * RET_QK_WIDTH + 2 * RET_WIDTH

MLA_HEADS = 8
MLA_NOPE = 128
MLA_ROPE = 64
MLA_V = 128
MLA_WIDTH = MLA_HEADS * MLA_V
Q_LORA = 384
KV_LORA = 256
MLA_IN = Q_LORA + MLA_WIDTH


def rmsnorm(x, g):
    xf = x.astype(jnp.float32)
    y = xf * lax.rsqrt(jnp.mean(xf * xf, axis=-1, keepdims=True) + RMS_EPS)
    return (y * g.astype(jnp.float32)).astype(x.dtype)

def rope(x, pos):
    half = x.shape[-1] // 2
    inv = ROPE_BASE ** (-jnp.arange(half, dtype=jnp.float32) / half)
    ang = pos.astype(jnp.float32)[:, None] * inv[None, :]
    cos = jnp.cos(ang)[None, :, None, :].astype(x.dtype)
    sin = jnp.sin(ang)[None, :, None, :].astype(x.dtype)
    x1, x2 = x[..., :half], x[..., half:]
    return jnp.concatenate([x1 * cos - x2 * sin, x1 * sin + x2 * cos], axis=-1)

def retention_decays(dtype):
    log_g = jnp.log(1.0 - jnp.exp2(-5.0 - jnp.arange(RET_HEADS, dtype=jnp.float32)))
    idx = jnp.arange(CHUNK, dtype=jnp.float32)
    dist = jnp.abs(idx[:, None] - idx[None, :])
    inner = jnp.exp(log_g[:, None, None] * dist[None])
    xi = jnp.exp(log_g[:, None] * (idx + 1.0)[None])
    zeta = jnp.exp(log_g[:, None] * (CHUNK - 1.0 - idx)[None])
    g_c = jnp.exp(log_g * CHUNK)
    return inner.astype(dtype), xi.astype(dtype), zeta.astype(dtype), g_c.astype(dtype)

def retention_layer(x, g_pre, w_in, gn_gain, w_out, g_post):
    b, s, _ = x.shape
    nc = s // CHUNK
    h = rmsnorm(x, g_pre)
    proj = h @ w_in
    q, k, v, gate = jnp.split(proj, [RET_QK_WIDTH, 2 * RET_QK_WIDTH, 2 * RET_QK_WIDTH + RET_WIDTH], axis=-1)
    pos = jnp.arange(s)
    q = rope(q.reshape(b, s, RET_HEADS, RET_QK_DIM), pos)
    k = rope(k.reshape(b, s, RET_HEADS, RET_QK_DIM), pos) * (RET_QK_DIM ** -0.5)
    v = v.reshape(b, s, RET_HEADS, RET_V_DIM)

    def to_chunks(t):
        return t.reshape(b, nc, CHUNK, RET_HEADS, t.shape[-1]).transpose(1, 0, 3, 2, 4)

    qc, kc, vc = to_chunks(q), to_chunks(k), to_chunks(v)
    inner_dec, xi, zeta, g_c = retention_decays(x.dtype)
    scores = jnp.einsum('nbhcd,nbhmd->nbhcm', qc, kc) * inner_dec[None, None]
    inner = jnp.einsum('nbhcm,nbhme->nbhce', scores, vc)

    def step(R, inp):
        q_i, k_i, v_i = inp
        cross = jnp.einsum('bhcd,bhde->bhce', q_i, R) * xi[None, :, :, None]
        R = R * g_c[None, :, None, None] + jnp.einsum('bhcd,bhce->bhde', k_i * zeta[None, :, :, None], v_i)
        return R, cross

    R0 = jnp.zeros((b, RET_HEADS, RET_QK_DIM, RET_V_DIM), x.dtype)
    _, cross = lax.scan(step, R0, (qc, kc, vc))
    o = (inner + cross).transpose(1, 0, 3, 2, 4).reshape(b, s, RET_HEADS, RET_V_DIM)
    of = o.astype(jnp.float32)
    mu = jnp.mean(of, axis=-1, keepdims=True)
    var = jnp.mean(jnp.square(of - mu), axis=-1, keepdims=True)
    o = ((of - mu) * lax.rsqrt(var + RMS_EPS)).reshape(b, s, RET_WIDTH) * gn_gain.astype(jnp.float32)
    y = (jax.nn.silu(gate) * o.astype(x.dtype)) @ w_out
    return x + rmsnorm(y, g_post)

def shared_latent_kv(h, g_kv, w_kv_a, g_kv_lat, w_uk, w_uv):
    b, s, _ = h.shape
    src = rmsnorm(h, g_kv)
    a = src @ w_kv_a
    c_kv, k_r = a[..., :KV_LORA], a[..., KV_LORA:]
    c_kv = rmsnorm(c_kv, g_kv_lat)
    k_nope = (c_kv @ w_uk).reshape(b, s, MLA_HEADS, MLA_NOPE)
    v = (c_kv @ w_uv).reshape(b, s, MLA_HEADS, MLA_V)
    k_rope = rope(k_r[:, :, None, :], jnp.arange(s))[:, :, 0, :]
    return k_nope, k_rope, v

def mla_attention(q_nope, q_rope, k_nope, k_rope, v):
    b, s = q_nope.shape[:2]
    nb = s // Q_BLOCK
    qn = q_nope.reshape(b, nb, Q_BLOCK, MLA_HEADS, MLA_NOPE).transpose(1, 0, 2, 3, 4)
    qr = q_rope.reshape(b, nb, Q_BLOCK, MLA_HEADS, MLA_ROPE).transpose(1, 0, 2, 3, 4)
    k_chunk = jnp.arange(s) // CHUNK
    scale = (MLA_NOPE + MLA_ROPE) ** -0.5

    def block(args):
        qn_i, qr_i, i = args
        sc = jnp.einsum('bqhd,bkhd->bhqk', qn_i, k_nope) + jnp.einsum('bqhr,bkr->bhqk', qr_i, k_rope)
        sc = sc.astype(jnp.float32) * scale
        q_chunk = (i * Q_BLOCK + jnp.arange(Q_BLOCK)) // CHUNK
        mask = k_chunk[None, :] <= q_chunk[:, None]
        sc = jnp.where(mask[None, None], sc, -jnp.inf)
        p = jax.nn.softmax(sc, axis=-1).astype(v.dtype)
        return jnp.einsum('bhqk,bkhd->bqhd', p, v)

    out = lax.map(block, (qn, qr, jnp.arange(nb)))
    return out.transpose(1, 0, 2, 3, 4).reshape(b, s, MLA_WIDTH)

def mla_layer(x, g_pre, w_in, g_q_lat, w_uq, w_out, g_post, k_nope, k_rope, v):
    b, s, _ = x.shape
    h = rmsnorm(x, g_pre)
    proj = h @ w_in
    c_q, gate = proj[..., :Q_LORA], proj[..., Q_LORA:]
    q = (rmsnorm(c_q, g_q_lat) @ w_uq).reshape(b, s, MLA_HEADS, MLA_NOPE + MLA_ROPE)
    q_nope = q[..., :MLA_NOPE]
    q_rope = rope(q[..., MLA_NOPE:], jnp.arange(s))
    o = mla_attention(q_nope, q_rope, k_nope, k_rope, v)
    y = (jax.nn.silu(gate) * o) @ w_out
    return x + rmsnorm(y, g_post)

def first_inputs(seed: int = 0) -> dict:
    key = jax.random.key(seed)
    ks = jax.random.split(key, 20)
    n_a = DEPTH // 2
    n_b = DEPTH - n_a
    f32 = jnp.float32

    def w(k, shape, fan_in):
        return jax.random.normal(k, shape, f32) * (fan_in ** -0.5)

    def gain(k, shape):
        return 1.0 + 0.02 * jax.random.normal(k, shape, f32)

    return {
        'x': jax.random.normal(ks[0], (BATCH, SEQ, D_MODEL), f32),
        'g_pre_a': gain(ks[1], (n_a, D_MODEL)),
        'w_in_a': w(ks[2], (n_a, D_MODEL, RET_IN), D_MODEL),
        'gn_gain_a': gain(ks[3], (n_a, RET_WIDTH)),
        'w_out_a': w(ks[4], (n_a, RET_WIDTH, D_MODEL), RET_WIDTH),
        'g_post_a': gain(ks[5], (n_a, D_MODEL)),
        'g_kv': gain(ks[6], (D_MODEL,)),
        'w_kv_a': w(ks[7], (D_MODEL, KV_LORA + MLA_ROPE), D_MODEL),
        'g_kv_lat': gain(ks[8], (KV_LORA,)),
        'w_uk': w(ks[9], (KV_LORA, MLA_HEADS * MLA_NOPE), KV_LORA),
        'w_uv': w(ks[10], (KV_LORA, MLA_WIDTH), KV_LORA),
        'g_pre_b': gain(ks[11], (n_b, D_MODEL)),
        'w_in_b': w(ks[12], (n_b, D_MODEL, MLA_IN), D_MODEL),
        'g_q_lat': gain(ks[13], (n_b, Q_LORA)),
        'w_uq': w(ks[14], (n_b, Q_LORA, MLA_HEADS * (MLA_NOPE + MLA_ROPE)), Q_LORA),
        'w_out_b': w(ks[15], (n_b, MLA_WIDTH, D_MODEL), MLA_WIDTH),
        'g_post_b': gain(ks[16], (n_b, D_MODEL)),
    }

def first_block(x, g_pre_a, w_in_a, gn_gain_a, w_out_a, g_post_a, g_kv, w_kv_a, g_kv_lat, w_uk, w_uv,
              g_pre_b, w_in_b, g_q_lat, w_uq, w_out_b, g_post_b):
    n_a = w_in_a.shape[0]
    h = x
    k_nope = k_rope = v = None
    for layer in range(DEPTH):
        if layer < n_a:
            h = retention_layer(h, g_pre_a[layer], w_in_a[layer], gn_gain_a[layer], w_out_a[layer], g_post_a[layer])
        else:
            if layer == n_a:
                k_nope, k_rope, v = shared_latent_kv(h, g_kv, w_kv_a, g_kv_lat, w_uk, w_uv)
            j = layer - n_a
            h = mla_layer(h, g_pre_b[j], w_in_b[j], g_q_lat[j], w_uq[j], w_out_b[j], g_post_b[j], k_nope, k_rope, v)
    return h


N_A_LAYERS = DEPTH // 2
N_B_LAYERS = DEPTH - N_A_LAYERS
CONV_WIDTH = 3
N_HEADS = 8
HEAD_DIM = D_MODEL // (2 * N_HEADS)
V_HEAD_DIM = 2 * HEAD_DIM
QK_WIDTH = N_HEADS * 2 * HEAD_DIM
V_WIDTH = N_HEADS * V_HEAD_DIM
D_FF = ((8 * D_MODEL // 3 + 127) // 128) * 128
PLE_DIM = 256
N_BUCKETS = 32
MAX_DISTANCE = 128
EPS = 1e-6


def rms_norm(x, g):
    xf = x.astype(jnp.float32)
    y = xf * lax.rsqrt(jnp.mean(xf * xf, axis=-1, keepdims=True) + EPS)
    return (y * g.astype(jnp.float32)).astype(x.dtype)

def causal_dwconv(x, w):
    c = x.shape[-1]
    return lax.conv_general_dilated(
        x, w[:, None, :].astype(x.dtype), window_strides=(1,),
        padding=[(CONV_WIDTH - 1, 0)], dimension_numbers=('NWC', 'WIO', 'NWC'),
        feature_group_count=c)

def rel_bucket(dist):
    max_exact = N_BUCKETS // 2
    large = max_exact + (jnp.log(jnp.maximum(dist, 1).astype(jnp.float32) / max_exact)
                         / math.log(MAX_DISTANCE / max_exact)
                         * (N_BUCKETS - max_exact)).astype(jnp.int32)
    large = jnp.minimum(large, N_BUCKETS - 1)
    return jnp.where(dist < max_exact, dist, large)

def short_conv_mixer(h, w_in, w_conv, w_out):
    gb, gc, u = jnp.split(h @ w_in, 3, axis=-1)
    return (gb * causal_dwconv(gc * u, w_conv)) @ w_out

def conv_ffn(h, w_up, w_conv, w_down):
    gate, up = jnp.split(causal_dwconv(h @ w_up, w_conv), 2, axis=-1)
    return (jax.nn.silu(gate) * up) @ w_down

def per_layer_embed(x, p_i, g_pre, w_gate, w_proj, g_post):
    gate = jax.nn.sigmoid(rms_norm(x, g_pre) @ w_gate)
    return rms_norm(gate * (p_i @ w_proj), g_post)

def shared_kv(x, g_kv, w_kv):
    b, s, _ = x.shape
    k, v = jnp.split(rms_norm(x, g_kv) @ w_kv, [QK_WIDTH], axis=-1)
    return (k.reshape(b, s, N_HEADS, 2, HEAD_DIM),
            v.reshape(b, s, N_HEADS, V_HEAD_DIM))

def diff_attention(h, k, v, dist_bias, w_q, lam_vecs, subln_g, w_o, lambda_init):
    b, s, _ = h.shape
    nb = s // Q_BLOCK
    q = (h @ w_q).reshape(b, nb, Q_BLOCK, N_HEADS, 2, HEAD_DIM).transpose(1, 0, 2, 3, 4, 5)
    lv = lam_vecs.astype(jnp.float32)
    lam = jnp.exp(jnp.sum(lv[0] * lv[1])) - jnp.exp(jnp.sum(lv[2] * lv[3])) + lambda_init
    kf = k.astype(jnp.float32)
    vf = v.astype(jnp.float32)
    bias_tab = dist_bias.astype(jnp.float32)
    k_pos = jnp.arange(s)
    scale = HEAD_DIM ** -0.5

    def block(args):
        qb, blk = args
        q_pos = blk * Q_BLOCK + jnp.arange(Q_BLOCK)
        dist = q_pos[:, None] - k_pos[None, :]
        bias = jnp.take(bias_tab, jnp.maximum(dist, 0), axis=0).transpose(2, 0, 1)
        logits = jnp.einsum('bqhmd,bkhmd->bhmqk', qb.astype(jnp.float32), kf) * scale
        logits = logits + bias[None, :, None]
        logits = jnp.where((dist >= 0)[None, None, None], logits, -jnp.inf)
        probs = jax.nn.softmax(logits, axis=-1)
        attn = probs[:, :, 0] - lam * probs[:, :, 1]
        return jnp.einsum('bhqk,bkhe->bqhe', attn, vf)

    o = lax.map(block, (q, jnp.arange(nb)))
    o = o.transpose(1, 0, 2, 3, 4).reshape(b, s, N_HEADS, V_HEAD_DIM)
    o = rms_norm(o, subln_g) * (1.0 - lambda_init)
    return o.reshape(b, s, V_WIDTH).astype(h.dtype) @ w_o

def second_inputs(seed: int = 0) -> dict:
    key = jax.random.key(seed)
    ks = jax.random.split(key, 24)
    f32 = jnp.float32

    def nrm(k, shape, scale):
        return jax.random.normal(k, shape, f32) * scale

    def gain(k, shape):
        return 1.0 + 0.05 * jax.random.normal(k, shape, f32)

    return {
        "x": nrm(ks[0], (BATCH, SEQ, D_MODEL), 1.0),
        "p": nrm(ks[1], (DEPTH, BATCH, SEQ, PLE_DIM), 1.0),
        "g_pre_mix": gain(ks[2], (DEPTH, D_MODEL)),
        "g_post_mix": gain(ks[3], (DEPTH, D_MODEL)),
        "g_pre_ffn": gain(ks[4], (DEPTH, D_MODEL)),
        "g_post_ffn": gain(ks[5], (DEPTH, D_MODEL)),
        "g_pre_ple": gain(ks[6], (DEPTH, D_MODEL)),
        "g_post_ple": gain(ks[7], (DEPTH, D_MODEL)),
        "w_sc_in": nrm(ks[8], (N_A_LAYERS, D_MODEL, 3 * D_MODEL), D_MODEL ** -0.5),
        "w_sc_conv": nrm(ks[9], (N_A_LAYERS, CONV_WIDTH, D_MODEL), CONV_WIDTH ** -0.5),
        "w_sc_out": nrm(ks[10], (N_A_LAYERS, D_MODEL, D_MODEL), D_MODEL ** -0.5),
        "g_kv": gain(ks[11], (D_MODEL,)),
        "w_kv": nrm(ks[12], (D_MODEL, QK_WIDTH + V_WIDTH), D_MODEL ** -0.5),
        "rel_bias": nrm(ks[13], (N_BUCKETS, N_HEADS), 0.5),
        "w_q": nrm(ks[14], (N_B_LAYERS, D_MODEL, QK_WIDTH), D_MODEL ** -0.5),
        "diff_lambda": nrm(ks[15], (N_B_LAYERS, 4, HEAD_DIM), 0.1),
        "g_subln": gain(ks[16], (N_B_LAYERS, V_HEAD_DIM)),
        "w_o": nrm(ks[17], (N_B_LAYERS, V_WIDTH, D_MODEL), V_WIDTH ** -0.5),
        "w_ffn_up": nrm(ks[18], (DEPTH, D_MODEL, 2 * D_FF), D_MODEL ** -0.5),
        "w_ffn_conv": nrm(ks[19], (DEPTH, CONV_WIDTH, 2 * D_FF), CONV_WIDTH ** -0.5),
        "w_ffn_down": nrm(ks[20], (DEPTH, D_FF, D_MODEL), D_FF ** -0.5),
        "w_ple_gate": nrm(ks[21], (DEPTH, D_MODEL, D_MODEL), D_MODEL ** -0.5),
        "w_ple_proj": nrm(ks[22], (DEPTH, PLE_DIM, D_MODEL), PLE_DIM ** -0.5),
    }

def second_block(x, p, g_pre_mix, g_post_mix, g_pre_ffn, g_post_ffn, g_pre_ple, g_post_ple,
              w_sc_in, w_sc_conv, w_sc_out, g_kv, w_kv, rel_bias, w_q, diff_lambda,
              g_subln, w_o, w_ffn_up, w_ffn_conv, w_ffn_down, w_ple_gate, w_ple_proj):
    s = x.shape[1]
    dist_bias = jnp.take(rel_bias, rel_bucket(jnp.arange(s)), axis=0)
    k = None
    v = None
    for i in range(DEPTH):
        h = rms_norm(x, g_pre_mix[i])
        if i < N_A_LAYERS:
            mix = short_conv_mixer(h, w_sc_in[i], w_sc_conv[i], w_sc_out[i])
        else:
            j = i - N_A_LAYERS
            if j == 0:
                k, v = shared_kv(x, g_kv, w_kv)
            lambda_init = 0.8 - 0.6 * math.exp(-0.3 * i)
            mix = diff_attention(h, k, v, dist_bias, w_q[j], diff_lambda[j], g_subln[j],
                                 w_o[j], lambda_init)
        x = x + rms_norm(mix, g_post_mix[i])
        ffn = conv_ffn(rms_norm(x, g_pre_ffn[i]), w_ffn_up[i], w_ffn_conv[i], w_ffn_down[i])
        x = x + rms_norm(ffn, g_post_ffn[i])
        x = x + per_layer_embed(x, p[i], g_pre_ple[i], w_ple_gate[i], w_ple_proj[i], g_post_ple[i])
    return x


def setup_inputs(seed=0):
    out = dict(first_inputs(seed))
    for name, value in second_inputs(seed + 1).items():
        if name != "x":
            out[name + "_2"] = value
    return out


def reference(
    x, g_pre_a, w_in_a, gn_gain_a, w_out_a, g_post_a, g_kv, w_kv_a, g_kv_lat, w_uk, w_uv,
    g_pre_b, w_in_b, g_q_lat, w_uq, w_out_b, g_post_b, p_2, g_pre_mix_2, g_post_mix_2,
    g_pre_ffn_2, g_post_ffn_2, g_pre_ple_2, g_post_ple_2, w_sc_in_2, w_sc_conv_2, w_sc_out_2,
    g_kv_2, w_kv_2, rel_bias_2, w_q_2, diff_lambda_2, g_subln_2, w_o_2, w_ffn_up_2,
    w_ffn_conv_2, w_ffn_down_2, w_ple_gate_2, w_ple_proj_2,
):
    x = first_block(
        x, g_pre_a, w_in_a, gn_gain_a, w_out_a, g_post_a, g_kv, w_kv_a, g_kv_lat, w_uk, w_uv,
        g_pre_b, w_in_b, g_q_lat, w_uq, w_out_b, g_post_b,
    )
    return second_block(
        x, p_2, g_pre_mix_2, g_post_mix_2, g_pre_ffn_2, g_post_ffn_2, g_pre_ple_2, g_post_ple_2,
        w_sc_in_2, w_sc_conv_2, w_sc_out_2, g_kv_2, w_kv_2, rel_bias_2, w_q_2, diff_lambda_2,
        g_subln_2, w_o_2, w_ffn_up_2, w_ffn_conv_2, w_ffn_down_2, w_ple_gate_2, w_ple_proj_2,
    )


_drawn_inputs = setup_inputs


def setup_inputs(seed=0):
    import zlib

    import numpy as np

    out = dict(_drawn_inputs(seed))
    spreads = {}
    factors = {'g_q_lat': 3.591,
     'g_post_b': 3.555,
     'g_pre_ple_2': 19.901,
     'g_post_mix_2': 3.103,
     'g_post_ffn_2': 3.372,
     'g_post_ple_2': 3.399,
     'g_kv_2': 3.153,
     'g_subln_2': 4.283}
    for name, (base, spread) in spreads.items():
        noise = np.random.default_rng([zlib.crc32(name.encode()), seed]).standard_normal(out[name].shape)
        drawn = base * np.exp(spread * noise) if base else spread * noise
        out[name] = __import__('jax').numpy.asarray(drawn.astype(out[name].dtype))
    for name, factor in factors.items():
        out[name] = (out[name] * factor).astype(out[name].dtype)
    return out
```

```python
import math

import numpy as np

import concourse.bass as bass
from concourse import mybir

F32 = mybir.dt.float32
F32R = mybir.dt.float32r
I32 = mybir.dt.int32
ALU = mybir.AluOpType
ACT = mybir.ActivationFunctionType
AXX = mybir.AxisListType.X

P = 128
S = 512
KD = 8
EPS = 1e-6
UNIT = 8
RING = 4
AHEAD = 2
STAGES = 3
NF = 22
MAGIC = float(0x5F3759DF)
LAMBDA_INIT = 0.8 - 0.6 * math.exp(-0.3)
NEG = -1.0e30
TW = 640

COLS = {}
_at = 0
for _name, _n in (("g_pre_a", 8), ("gn_gain_a", 16), ("g_post_a", 8), ("g_kv", 8), ("g_kv_lat", 2), ("g_pre_b", 8),
                  ("g_q_lat", 3), ("g_post_b", 8), ("g_pre_mix_2", 16), ("g_post_mix_2", 16), ("g_pre_ffn_2", 16),
                  ("g_post_ffn_2", 16), ("g_pre_ple_2", 16), ("g_post_ple_2", 16), ("w_sc_conv_2", 24),
                  ("g_kv_2", 8), ("g_subln_2", 1), ("w_ffn_conv_2", 264)):
    COLS[_name] = _at
    _at += _n
NCOL = _at


class Slot:

    def __init__(self, ap, sem):
        self.ap, self.sem = ap, sem


class Ring:
    def __init__(self, slots):
        self.slots, self.n = slots, 0

    def next(self):
        b = self.slots[self.n % len(self.slots)]
        self.n += 1
        return b


class Engine:

    def __init__(self, counts):
        self.steps, self.counts = [], counts

    def wait(self, *marks):
        self.steps += [(None, m[0], m[1]) for m in marks if m is not None and m[1] > 0]
        return self

    def do(self, fn, sig=None, inc=1):
        if sig is not None:
            self.counts[sig] = self.counts.get(sig, 0) + inc
        self.steps.append((fn, sig, inc))
        return sig, self.counts.get(sig, 0)

    def dma(self, out, in_, sig):
        return self.do(lambda e: e.dma_start(out, in_), sig, 16)

    def act(self, out, in_, scale=1.0, func=ACT.Copy, bias=0.0, accum=None, sig=None):
        if accum is None:
            return self.do(lambda e: e.activation(out, in_, func, bias=bias, scale=scale), sig)
        return self.do(lambda e: e.activation(out, in_, func, bias=bias, scale=scale, accum_out=accum), sig)

    def tt(self, out, a, b, op, sig=None):
        return self.do(lambda e: e.tensor_tensor(out, a, b, op), sig)

    def stt(self, out, a, s, b, op0, op1, sig=None):
        return self.do(lambda e: e.scalar_tensor_tensor(out=out, in0=a, scalar=s, in1=b, op0=op0, op1=op1), sig)

    def ts(self, out, a, s1, s2, op0, op1=None, sig=None):
        if s2 is None:
            return self.do(lambda e: e.tensor_scalar(out, a, s1, None, op0), sig)
        return self.do(lambda e: e.tensor_scalar(out, a, s1, s2, op0, op1), sig)

    def mm(self, out, lhsT, rhs, start, stop, sig=None):
        return self.do(lambda e: e.matmul(out, lhsT, rhs, start=start, stop=stop), sig)

    def turn(self, out, in_, ident, sig=None):
        return self.do(lambda e: e.transpose(out, in_, ident), sig)

    def issue(self, e, sems):
        for fn, sig, n in self.steps:
            if fn is None:
                e.wait_ge(sems[sig], n)
            else:
                ins = fn(e)
                if sig is not None:
                    ins.then_inc(sems[sig], n)


class Net:
    def __init__(self, nc, ctx, ins, out):
        self.nc, self.ctx, self.ins, self.out = nc, ctx, ins, out
        self.counts = {}
        self.pe, self.act, self.dve, self.pool, self.sp = (Engine(self.counts) for _ in range(5))
        self.order = []
        self.NU = ins["ws"].shape[0] // P
        self.alloc()

    def alloc(self):
        nc, ctx = self.nc, self.ctx

        def sb(name, n, dt):
            return ctx.enter_context(nc.sbuf_tensor(name, [P, n], dt))

        self.WH = sb("WH", RING * 1024, F32R)
        self.WL = sb("WL", RING * 1024, F32R)
        self.stage = sb("stage", STAGES * 1024, F32)
        self.FR = sb("FR", 8192 + 23040, F32R)
        self.MK = self.FR[:, 8192 + 22528:8192 + 22784]
        self.X = sb("X", 4096, F32)
        self.R = sb("R", 512, F32)
        self.R2 = sb("R2", 512, F32)
        self.T = sb("T", 6 * 512, F32)
        self.FD = sb("FD", 5120, F32)
        self.cols = sb("cols", NCOL, F32)
        self.ident = sb("ident", 128, F32)
        self.ones = sb("ones", 2, F32)
        self.sm = sb("sm", 160, F32)
        self.held = sb("held", 72, F32)
        self.keep = sb("keep", 24, F32)
        self.masks = sb("masks", 2, F32)
        self.acc = sb("acc", 512, F32)
        self.bank = [Slot(ctx.enter_context(nc.psum_tensor(f"pb{i}", [P, 512], F32))[:, :], f"bank{i}")
                     for i in range(8)]
        self.tmp = Ring([Slot(self.T[:, 512 * i:512 * i + 512], f"tmp{i}") for i in range(6)])
        self.smn = self.nheld = 0
        self.Y = [self.FD[:, 512 * m:512 * m + 512] for m in range(8)]

    def small(self, n):
        if self.smn + n > 160:
            self.smn = 0
        a = self.sm[:, self.smn:self.smn + n]
        self.smn += n
        return a

    def xt(self, k):
        return self.X[:, 512 * k:512 * k + 512]

    def xin(self, part, k):
        return self.FR[:, part * 4096 + 512 * k:part * 4096 + 512 * k + 512]

    def col(self, name, i):
        c = COLS[name] + i
        return self.cols[:, c:c + 1]

    def count(self, sem):
        return sem, self.counts.get(sem, 0)

    def freed(self, slot):
        return self.count(slot.sem)

    def stream_start(self):
        self.loads = self.splits = 0
        self.loaded, self.unit_ready, self.unit_end, self.pe_at = [], [], {}, -1
        for _ in range(STAGES):
            self.load_unit()

    def load_unit(self):
        u = self.loads
        if u >= self.NU:
            return
        self.loads += 1
        s = u % STAGES
        if u >= STAGES:
            self.sp.wait(self.unit_ready[u - STAGES])
        self.loaded.append(self.sp.dma(self.stage[:, 1024 * s:1024 * s + 1024], self.ins["ws"][P * u:P * u + P, :],
                                       f"load{s}"))

    def split_unit(self):
        u = self.splits
        self.splits += 1
        s, w = u % STAGES, u % RING
        src = self.stage[:, 1024 * s:1024 * s + 1024]
        hi, lo = self.WH[:, 1024 * w:1024 * w + 1024], self.WL[:, 1024 * w:1024 * w + 1024]
        used = self.unit_end[u - RING] if u >= RING else None
        a = self.act.wait(self.loaded[u], used).act(hi, src, sig="w_hi")
        self.unit_ready.append(self.dve.wait(a).tt(lo, src, hi.bitcast(F32), ALU.subtract, sig="w_lo"))
        self.load_unit()

    def blocks(self, specs):
        at = len(self.order)
        self.order += specs
        u, o = at // UNIT, 128 * (at % UNIT)
        n = 128 * len(specs)
        assert o + n <= 128 * UNIT
        while self.splits <= min(u + AHEAD, self.NU - 1):
            self.split_unit()
        w = 1024 * (u % RING) + o
        return self.WH[:, w:w + n], self.WL[:, w:w + n], u

    def pe_unit(self, u):
        if u > self.pe_at:
            self.pe.wait(self.unit_ready[u])
            self.pe_at = u

    def group(self, out, terms, first=True, last=True, sig=None):
        n = len(terms)
        for i, (l, r) in enumerate(terms):
            mark = self.pe.mm(out, l, r, first and i == 0, last and i == n - 1, sig if i == n - 1 else None)
        return mark

    def proj(self, name, cols, K, xin, bank, ready=None):
        self.pe.wait(self.freed(bank))
        for k in range(K):
            wh, wl, u = self.blocks([(name, k, cols)])
            self.pe_unit(u)
            if ready:
                self.pe.wait(ready[k])
            mark = self.group(bank.ap, [(wh, xin(0, k)), (wh, xin(1, k)), (wl, xin(0, k))], k == 0, k == K - 1,
                              "pe_proj")
            self.unit_end[u] = mark
        return mark

    def proj_wide(self, name, colsets, K, xin, banks, prepare):
        marks = [None] * len(colsets)
        ahead = [prepare(0)]
        for k in range(K):
            if k + 1 < K:
                ahead.append(prepare(k + 1))
            for n, cols in enumerate(colsets):
                if k == 0:
                    self.pe.wait(self.freed(banks[n]))
                wh, wl, u = self.blocks([(name, k, cols)])
                self.pe_unit(u)
                if n == 0:
                    self.pe.wait(ahead[k])
                marks[n] = self.group(banks[n].ap, [(wh, xin(0, k)), (wh, xin(1, k)), (wl, xin(0, k))],
                                      k == 0, k == K - 1, "pe_proj")
                self.unit_end[u] = marks[n]
        return marks

    def proj_nat(self, name, wide, K, xin, ring, ready=None):
        bl = [self.blocks([(name, k, c) for c in wide]) for k in range(K)]
        outs = []
        for p in range(2):
            bank = ring.next()
            self.pe.wait(self.freed(bank))
            for t in (2 * p, 2 * p + 1):
                sl = slice(128 * t, 128 * t + 128)
                ap = bank.ap[:, 256 * (t % 2):256 * (t % 2) + 256]
                for k in range(K):
                    wh, wl, u = bl[k]
                    self.pe_unit(u)
                    if ready:
                        self.pe.wait(ready[k])
                    mark = self.group(ap, [(xin(0, k)[:, sl], wh), (xin(0, k)[:, sl], wl), (xin(1, k)[:, sl], wh)],
                                      k == 0, k == K - 1, "pe_proj")
                    self.unit_end[u] = mark
            outs.append((bank, mark))
        return outs

    def tokens_out(self, outs, y, yw, dst, reuse):
        for p, (bank, mark) in enumerate(outs):
            self.act.wait(mark, yw, reuse)
            for t in (2 * p, 2 * p + 1):
                a = self.act.act(dst(t)[0], bank.ap[:, 256 * (t % 2):256 * (t % 2) + 256], scale=y[:, t:t + 1],
                                 sig="tok_hi")
            self.dve.wait(a)
            for t in (2 * p, 2 * p + 1):
                hi, lo = dst(t)
                d = self.dve.stt(lo, bank.ap[:, 256 * (t % 2):256 * (t % 2) + 256], y[:, t:t + 1], hi.bitcast(F32),
                                 ALU.mult, ALU.subtract, sig=bank.sem if t % 2 else None)
        return d

    def newton(self, a, y, after, out_scale=1.0):
        dve = self.dve
        t = self.small(a.shape[-1])
        m = dve.wait(after).ts(t.bitcast(I32), a.bitcast(I32), 1, None, ALU.logical_shift_right, sig="newton")
        m = dve.wait(m).ts(y.bitcast(I32), t.bitcast(I32), -1.0, MAGIC, ALU.mult, ALU.add, sig="newton")
        for i in range(3):
            m = dve.wait(m).tt(t, y, y, ALU.mult, sig="newton")
            m = dve.wait(m).stt(t, t, -0.5, a, ALU.mult, ALU.mult, sig="newton")
            m = dve.wait(m).stt(y, t, 1.5, y, ALU.add, ALU.mult, sig="newton")
        if out_scale != 1.0:
            m = dve.wait(m).ts(y, y, out_scale, None, ALU.mult, sig="newton")
        return m

    def square(self, first, src, after, sig="sq"):
        if first:
            self.acc_mark = self.act.wait(after).act(self.acc[:, :], src, func=ACT.Square, sig=sig)
            return self.acc_mark
        t = self.tmp.next()
        a = self.act.wait(after, self.freed(t)).act(t.ap, src, func=ACT.Square, sig=sig)
        self.acc_mark = self.pool.wait(a, self.acc_mark).tt(self.acc[:, :], self.acc[:, :], t.ap, ALU.add, sig=t.sem)
        return self.acc_mark

    def token_sums(self, after, more=None):
        b = self.bank[7]
        self.pe.wait(after, self.freed(b))
        for c in range(4):
            sl = slice(128 * c, 128 * c + 128)
            m = self.pe.mm(b.ap[:, c:c + 1], self.acc[:, sl], self.ones[:, 0:1], True, more is None, sig="pe_sums")
            if more is not None:
                if c == 0:
                    self.pe.wait(more[1])
                m = self.pe.mm(b.ap[:, c:c + 1], more[0].ap[:, sl], self.ones[:, 0:1], False, True,
                               sig=more[0].sem if c == 3 else "pe_sums")
        return m

    def rms(self, sums, D, out_scale=1.0):
        a, y = self.small(4), self.held[:, self.nheld:self.nheld + 4]
        self.nheld += 4
        m = self.dve.wait(sums).ts(a, self.bank[7].ap[:, 0:4], 1.0 / D, EPS, ALU.mult, ALU.add, sig=self.bank[7].sem)
        return y, self.newton(a, y, m, out_scale)

    def spread(self, y, yw):
        b = self.bank[6]
        self.pe.wait(yw, self.freed(b))
        for c in range(4):
            m = self.pe.mm(b.ap[:, 128 * c:128 * c + 128], y[:, c:c + 1].broadcast_to([P, P]), self.ident[:, :],
                           True, True, sig="pe_spread")
        return m

    def stats(self, after, D, out):
        y, yw = self.rms(self.token_sums(after), D)
        m = self.spread(y, yw)
        return y, yw, out[:, :], self.act.wait(m).act(out[:, :], self.bank[6].ap, sig=self.bank[6].sem)

    def xg_tile(self, name, base, k, after, reuse=None):
        g = self.col(name, base + k)
        hi, lo = self.xin(0, k), self.xin(1, k)
        a = self.act.wait(after, reuse).act(hi, self.xt(k), scale=g, sig="xg_hi")
        return self.dve.wait(a, after).stt(lo, self.xt(k), g, hi.bitcast(F32), ALU.mult, ALU.subtract, sig="xg_lo")

    def out_tile(self, m, mark, bank, more=None):
        if m == 0:
            self.acc_mark = self.act.wait(mark).act(self.acc[:, :], bank.ap, func=ACT.Square, sig="sq")
        else:
            t = self.tmp.next()
            a = self.act.wait(mark, self.freed(t)).act(t.ap, bank.ap, func=ACT.Square, sig="sq")
            if m < 7:
                self.acc_mark = self.pool.wait(a, self.acc_mark).tt(self.acc[:, :], self.acc[:, :], t.ap, ALU.add, sig=t.sem)
            else:
                self.last_square = (t, a)
        self.y_mark = self.act.act(self.Y[m], bank.ap, sig=bank.sem)

    def out_proj(self, name, K, xin, ready, reuse, filler=None):
        self.act.wait(*reuse)
        ring = Ring(self.bank[0:6])
        wide = [ring.next() for _ in range(4)]
        marks = self.proj_wide(name, [0, 1, 2, 3], K, xin, wide, lambda k: ready[k])
        for m in range(8):
            if m < 4:
                b, mark = wide[m], marks[m]
            else:
                b = ring.next()
                mark = self.proj(name, m, K, xin, b)
            self.out_tile(m, mark, b)
        self.y_last = mark

    def normed(self, D, gname, gbase, out_scale=1.0, filler=()):
        filler = list(filler)
        if filler:
            filler.pop(0)()
        sums = self.token_sums(self.acc_mark, self.last_square)
        y, yw = self.rms(sums, D, out_scale)
        for f in filler:
            f()
        m = self.spread(y, yw)

        def residual(k):
            t = self.tmp.next()
            if k == 0:
                self.dve.wait(m, self.y_mark)
            a = self.dve.wait(self.freed(t)).stt(t.ap, self.Y[k], self.col(gname, gbase + k), self.bank[6].ap,
                                                 ALU.mult, ALU.mult, sig="y_normed")
            self.y_read = a
            if k == 7:
                self.bank6_read = a
            return self.dve.wait(a).tt(self.xt(k), self.xt(k), t.ap, ALU.add, sig=t.sem)

        return residual

    def into(self, residual, gname, gbase, reuse):

        def prepare(k):
            x = residual(k)
            g = self.xg_tile(gname, gbase, k, x, reuse if k == 0 else None)
            self.sq_mark = self.square(k == 0, self.xt(k), x)
            return g

        return prepare

    def tables(self, name, off, reuse):
        t = self.FD[:, off:off + 1024]
        return t, self.sp.wait(*reuse).dma(t, self.ins[name][:, :], "tables")

    def scaled_tables(self, t, w, R, rw):
        self.dve.wait(w, rw).tt(t[:, 0:512], t[:, 0:512], R, ALU.mult)
        return self.dve.tt(t[:, 512:1024], t[:, 512:1024], R, ALU.mult, sig="tab_scaled")

    def rope_out(self, mark, bank, tab, tabw):
        A, B = self.tmp.next(), self.tmp.next()
        C, Sn = tab[:, 0:512], tab[:, 512:1024]
        self.dve.wait(mark, tabw, self.freed(A), self.freed(B)).tt(A.ap, bank.ap, C, ALU.mult)
        self.dve.tt(B.ap[64:128, :], bank.ap[0:64, :], Sn[0:64, :], ALU.mult)
        m = self.dve.tt(B.ap[0:64, :], bank.ap[64:128, :], Sn[64:128, :], ALU.mult, sig=bank.sem)
        return A, self.pool.wait(m).tt(A.ap, A.ap, B.ap, ALU.add, sig=B.sem)

    def split(self, hi, lo, src, after, reuse=None, eng=None, sig="split"):
        a = self.act.wait(after, reuse).act(hi, src, sig="split_hi")
        return (eng or self.pool).wait(a).tt(lo, src, hi.bitcast(F32), ALU.subtract, sig=sig)

    def silu2(self, g, bank, mark, R, rw, reuse=None):
        t = self.tmp.next()
        z = self.dve.wait(mark, rw, reuse).tt(g, bank.ap, R, ALU.mult, sig=bank.sem)
        a = self.act.wait(z, self.freed(t)).act(t.ap, g, scale=0.5, func=ACT.Tanh, sig="tanh")
        return self.dve.wait(a).stt(g, t.ap, 1.0, g, ALU.add, ALU.mult, sig=t.sem)

    def retention(self, xw):
        FR, FD, dve, act, pe, sp = self.FR, self.FD, self.dve, self.act, self.pe, self.sp
        D0 = 8192
        qk = [FR[:, D0 + 512 * i:D0 + 512 * i + 512] for i in range(4)]
        V = FR[:, D0 + 2048:D0 + 4096]
        Sb = FR[:, D0 + 4096:D0 + 4096 + 2560]
        Z = FR[:, D0 + 6656:D0 + 6656 + 16384]
        offs = [0, 512, 896, 1152]
        tab, tw = self.tables("rope_a", 0, [])
        dec = [FD[:, 1024 + 512 * i:1536 + 512 * i] for i in range(2)]
        gates = [FD[:, 2048 + 512 * i:2560 + 512 * i] for i in range(4)]
        ON = FD[:, 4096:5120]
        gn = self.keep[:, 8:24]
        gnw = dve.wait(self.cold).ts(gn, self.cols[:, COLS["gn_gain_a"]:COLS["gn_gain_a"] + 16], 0.5, None, ALU.mult,
                                     sig="gn_half")
        pr, sr = Ring(self.bank[0:3]), Ring(self.bank[3:5])
        st, zw = {}, {}

        def prepare(k):
            g = self.xg_tile("g_pre_a", 0, k, xw[k])
            self.sq_mark = self.square(k == 0, self.xt(k), xw[k])
            return g

        def qk_out(n, mark, b):
            A, s = self.rope_out(mark, b, tab, st["tab"])
            return self.split(qk[2 * n], qk[2 * n + 1], A.ap, s, self.count("pe_scores"), sig=A.sem)

        def do_qk(h):
            st["qk"] = []
            for n in range(2):
                b = pr.next()
                mark = self.proj("w_in_a", h + 8 * n, KD, self.xin, b)
                st["qk"].append(qk_out(n, mark, b))

        def do_v(h):
            outs = self.proj_nat("w_in_a", [16 + 2 * h, 17 + 2 * h], KD, self.xin, pr)
            st["v"] = self.tokens_out(outs, st["y"], st["yw"], lambda t: (V[:, 256 * t:256 * t + 256],
                                                                         V[:, 1024 + 256 * t:1280 + 256 * t]),
                                      self.count("pe_values"))

        def do_gate(h):
            for e in range(2):
                b = pr.next()
                mark = self.proj("w_in_a", 32 + 2 * h + e, KD, self.xin, b)
                g = gates[2 * (h % 2) + e]
                st[("g", h, e)] = (g, self.silu2(g, b, mark, self.R[:, :], st["rw"]))

        def do_s(h):
            d = dec[h % 2]
            ld = sp.wait(st.get(("masked", h - 2))).dma(d, self.ins["decay"][P * h:P * h + P, :], "decay")
            pe.wait(*st["qk"])
            values = self.count("pe_values")
            for j in range(4):
                b = sr.next()
                n = 512 - 128 * j
                kh, kl = qk[2][:, 128 * j:128 * j + 128], qk[3][:, 128 * j:128 * j + 128]
                qh, ql = qk[0][:, 128 * j:512], qk[1][:, 128 * j:512]
                pe.wait(self.freed(b))
                mark = self.group(b.ap[:, 0:n], [(kh, qh), (kh, ql), (kl, qh)], sig="pe_scores")
                t = self.tmp.next()
                m = dve.wait(mark, ld, self.freed(t)).tt(t.ap[:, 0:n], b.ap[:, 0:n], d[:, 0:n], ALU.mult,
                                                         sig=b.sem)
                o = offs[j]
                st["s"] = self.split(Sb[:, o:o + n], Sb[:, 1280 + o:1280 + o + n], t.ap[:, 0:n], m, values, sig=t.sem)
                st[("s", j)] = st["s"]
            st[("masked", h)] = m

        def do_o(h):
            mv, var, rs = self.small(8), self.small(4), self.small(4)
            marks = []
            pe.wait(st["v"])
            for i in range(4):
                b = self.bank[5 + i // 2]
                if i % 2 == 0:
                    pe.wait(self.freed(b))
                terms = []
                for j in range(i + 1):
                    o = offs[j] + 128 * (i - j)
                    sh, sl = Sb[:, o:o + 128], Sb[:, 1280 + o:1280 + o + 128]
                    vh, vl = V[:, 256 * j:256 * j + 256], V[:, 1024 + 256 * j:1280 + 256 * j]
                    terms += [(sh, vh), (sl, vh), (sh, vl)]
                pe.wait(st[("s", i)])
                marks.append(self.group(b.ap[:, 256 * (i % 2):256 * (i % 2) + 256], terms, sig="pe_values"))
            for i in range(4):
                ap = self.bank[5 + i // 2].ap[:, 256 * (i % 2):256 * (i % 2) + 256]
                s6, m2 = self.small(6), mv[:, 2 * i:2 * i + 2]
                d = dve.wait(marks[i | 1]).do(lambda e, s6=s6, ap=ap: e.bn_stats(s6, ap), "bn")
                d = dve.wait(d).do(lambda e, s6=s6, m2=m2: e.bn_aggr(m2, s6), "bn")
            vs = mv.rearrange("p (i t) -> p i t", t=2)[:, :, 1]
            d = dve.wait(d).ts(var, vs, EPS, None, ALU.add, sig="bn")
            d = self.newton(var, rs, d)
            dve.wait(d, self.count("pe_turn_o"))
            for i in range(4):
                b = self.bank[5 + i // 2]
                d = dve.ts(ON[:, 256 * i:256 * i + 256], b.ap[:, 256 * (i % 2):256 * (i % 2) + 256],
                           mv[:, 2 * i:2 * i + 1], rs[:, i:i + 1], ALU.subtract, ALU.mult,
                           sig=b.sem if i % 2 else None)
            st["on"] = d

        def do_t(h):
            pe.wait(st["on"])
            for e in range(2):
                b = self.bank[7] if e == 0 else pr.next()
                pe.wait(self.freed(b))
                for i in range(4):
                    mark = pe.turn(b.ap[:, 128 * i:128 * i + 128], ON[:, 256 * i + 128 * e:256 * i + 128 * e + 128],
                                   self.ident[:, :], sig="pe_turn_o")
                g, z = st[("g", h, e)]
                t = self.tmp.next()
                k = 2 * h + e
                m = dve.wait(mark, z, gnw, self.freed(t)).stt(t.ap, b.ap, gn[:, k:k + 1], g, ALU.mult, ALU.mult,
                                                              sig=b.sem)
                zw[k] = self.split(Z[:, 512 * k:512 * k + 512], Z[:, 8192 + 512 * k:8704 + 512 * k], t.ap, m,
                                   sig=t.sem)

        wide = [pr.next() for _ in range(2)]
        marks = self.proj_wide("w_in_a", [0, 8], KD, self.xin, wide, prepare)
        st["y"], st["yw"], R, st["rw"] = self.stats(self.sq_mark, 1024, self.R)
        st["tab"] = self.scaled_tables(tab, tw, R, st["rw"])
        st["qk"] = [qk_out(n, marks[n], wide[n]) for n in range(2)]
        do_v(0)
        do_gate(0)
        for h in range(8):
            do_s(h)
            if h < 7:
                do_qk(h + 1)
            do_o(h)
            if h < 7:
                do_v(h + 1)
                do_gate(h + 1)
            do_t(h)
        self.out_proj("w_out_a", 16, lambda p, k: Z[:, 8192 * p + 512 * k:8192 * p + 512 * k + 512], zw,
                      [self.count("pe_turn_o"), zw[15]])

    def latent(self, residual):
        FR, FD, dve, act, pe, sp = self.FR, self.FD, self.dve, self.act, self.pe, self.sp
        D0 = 8192

        def fr(o, n):
            return FR[:, D0 + o:D0 + o + n]

        ckv, cq, kr = fr(0, 2048), fr(2048, 3072), fr(5120, 2048)
        kb = Ring([fr(7168 + 1024 * i, 1024) for i in range(2)])
        vb = Ring([fr(9216 + 2048 * i, 2048) for i in range(2)])
        qn = Ring([fr(13312 + 1024 * i, 1024) for i in range(2)])
        qr = Ring([fr(15360 + 1024 * i, 1024) for i in range(2)])
        pt = Slot(fr(17408, 4096), "pt")
        Z = FR[:, 0:8192]
        gate = [FD[:, 512 * i:512 * i + 512] for i in range(8)]
        scale = 192 ** -0.5
        tab, tw = self.tables("rope_b", 4096, [self.y_last])
        pr = Ring(self.bank[0:6])
        t = self.tmp.next()
        mk = sp.wait(self.freed(t)).dma(t.ap[:, 0:128], self.ins["mask"][:, :], "mask")
        act.wait(self.y_last, mk).act(self.MK[:, 0:128], self.ident[:, :])
        mkw = act.act(self.MK[:, 128:256], t.ap[:, 0:128], sig=t.sem)

        def scaled(c, name, m, hi, lo, after, sig):
            g = self.col(name, m)
            a = act.wait(after).act(hi, c, scale=g, sig="lat_hi")
            return dve.wait(a).stt(lo, c, g, hi.bitcast(F32), ALU.mult, ALU.subtract, sig=sig)

        wide = [pr.next() for _ in range(3)]
        ropec = [256 + i % 32 + 32 * (i // 64) for i in range(128)]
        marks = self.proj_wide("w_kv_a", [0, 1, ropec], KD, self.xin, wide,
                               self.into(residual, "g_kv", 0, self.y_last))
        xg_read = marks[2]
        y, yw, R, rw = self.stats(self.sq_mark, 1024, self.R)
        def prepare(k):
            return self.xg_tile("g_pre_b", 0, k, None, xg_read if k == 0 else None)

        cs, sq = [], None
        for m in range(2):
            c = self.tmp.next()
            z = dve.wait(marks[m], rw, self.freed(c)).tt(c.ap, wide[m].ap, R, ALU.mult, sig=wide[m].sem)
            sq = self.square(m == 0, c.ap, z)
            cs.append(scaled(c.ap, "g_kv_lat", m, ckv[:, 512 * m:512 * m + 512],
                             ckv[:, 1024 + 512 * m:1536 + 512 * m], z, c.sem))
        tabw = self.scaled_tables(tab, tw, R, rw)
        A, s = self.rope_out(marks[2], wide[2], tab, tabw)
        for par in range(2):
            o = 1024 * par
            hi, lo = kr[:, o:o + 512], kr[:, o + 512:o + 1024]
            mk = self.masks[:, par:par + 1]
            a = act.wait(s).act(hi, A.ap, scale=mk, sig="lat_hi")
            krw = dve.wait(a).stt(lo, A.ap, mk, hi.bitcast(F32), ALU.mult, ALU.subtract, sig=A.sem if par else None)
        wide = [pr.next() for _ in range(3)]
        marks = self.proj_wide("w_in_b", [0, 1, 2], KD, self.xin, wide, prepare)
        y2, y2w, R2, r2w = self.stats(sq, 256, self.R2)
        cqw, sq = [], None
        for m in range(3):
            c = self.tmp.next()
            z = dve.wait(marks[m], self.freed(c)).tt(c.ap, wide[m].ap, R, ALU.mult, sig=wide[m].sem)
            sq = self.square(m == 0, c.ap, z)
            cqw.append(scaled(c.ap, "g_q_lat", m, cq[:, 512 * m:512 * m + 512],
                              cq[:, 1536 + 512 * m:2048 + 512 * m], z, c.sem))
        gw = []
        tw2 = sp.wait(krw).dma(tab, self.ins["rope_b"][:, :], "tables")
        for m in range(8):
            b = pr.next()
            mark = self.proj("w_in_b", 3 + m, KD, self.xin, b)
            gw.append(self.silu2(gate[m], b, mark, R, rw, self.y_read if m == 0 else None))
            if m == 3:
                sums = self.token_sums(sq)
                y3, y3w = self.rms(sums, 384)
        xg_read = mark
        m = self.spread(y3, y3w)
        r3w = act.wait(m, gw[-1]).act(self.R[:, :], self.bank[6].ap, sig=self.bank[6].sem)
        R3 = self.R[:, :]
        tabw3 = self.scaled_tables(tab, tw2, R3, r3w)
        pr, srg = Ring(self.bank[0:2]), Ring(self.bank[2:5])
        ptr, ob = Ring(self.bank[5:7]), Ring(self.bank[7:8])

        def kin(p, k):
            return ckv[:, 1024 * p + 512 * k:1024 * p + 512 * k + 512]

        def qin(p, k):
            return cq[:, 1536 * p + 512 * k:1536 * p + 512 * k + 512]

        st, zw = {}, {}
        every, probs = self.tmp, Ring(self.tmp.slots[0:4])
        self.tmp = Ring(every.slots[4:6])

        def rope_pair(h):
            b = pr.next()
            c0 = [192 * (h + i // 32 % 2) + 128 + 32 * (i // 64) + i % 32 for i in range(128)]
            mark = self.proj("w_uq", c0, 3, qin, b, cqw)
            A, s = self.rope_out(mark, b, tab, tabw3)
            q = qr.next()
            st["qr"] = (q, self.split(q[:, 0:512], q[:, 512:1024], A.ap, s, st.get(("S", h - 3)), sig=A.sem))

        def value_pair(h):
            v = vb.next()
            outs = self.proj_nat("w_uv", [h, h + 1], 2, kin, pr, cs)
            st["v"] = (v, self.tokens_out(outs, y2, y2w, lambda t: (v[:, 256 * t:256 * t + 256],
                                                                    v[:, 1024 + 256 * t:1280 + 256 * t]),
                                          self.count("pt")))

        def head_tile(h, name, cols, K, xi, ready, ring, Rr, rr):
            b = pr.next()
            mark = self.proj(name, cols, K, xi, b, ready)
            t = self.tmp.next()
            d = dve.wait(mark, rr, self.freed(t)).tt(t.ap, b.ap, Rr, ALU.mult, sig=b.sem)
            o = ring.next()
            return o, self.split(o[:, 0:512], o[:, 512:1024], t.ap, d, st.get(("S", h - 2)), sig=t.sem)

        def project(h):
            if h % 2 == 0:
                for f in (rope_pair, value_pair) if len(self.order) % 2 else (value_pair, rope_pair):
                    f(h)
            st["k"] = head_tile(h, "w_uk", h, 2, kin, cs, kb, R2, r2w)
            st["q"] = head_tile(h, "w_uq", list(range(192 * h, 192 * h + 128)), 3, qin, cqw, qn, R3, r3w)
            st[h] = dict(st)

        def scores(h):
            (q, qw), (k, kw), (qq, qqw) = st[h]["q"], st[h]["k"], st[h]["qr"]
            o = 1024 * (h % 2)
            rs, nm = self.small(4), self.small(4)
            pe.wait(qw, kw, qqw, krw, mkw)
            for i in range(4):
                n = 128 * (i + 1)
                b = srg.next()
                sl = slice(128 * i, 128 * i + 128)
                qh, ql = q[:, sl], q[:, 512 + 128 * i:640 + 128 * i]
                rh, rl = qq[:, sl], qq[:, 512 + 128 * i:640 + 128 * i]
                kh, kl = k[:, 0:n], k[:, 512:512 + n]
                th, tl = kr[:, o:o + n], kr[:, o + 512:o + 512 + n]
                pe.wait(self.freed(b))
                terms = [(rh, th), (rh, tl), (rl, th), (qh, kh), (qh, kl)]
                self.group(b.ap[:, 0:n], terms, True, False)
                self.group(b.ap[:, n - 128:n], [(self.MK[:, 0:128], self.MK[:, 128:256])], False, False)
                mark = self.group(b.ap[:, 0:n], [(ql, kh)], False, True, "pe_scores")
                mx = self.small(1)
                d = dve.wait(mark).do(lambda e, mx=mx, b=b, n=n: e.tensor_reduce(mx, b.ap[:, 0:n], AXX, ALU.max),
                                      "row_max")
                d = dve.wait(d).ts(nm[:, i:i + 1], mx, -scale, None, ALU.mult, sig="row_max")
                t = probs.next()
                a = act.wait(d, self.freed(t)).act(t.ap[:, 0:n], b.ap[:, 0:n], scale=scale, func=ACT.Exp,
                                                   bias=nm[:, i:i + 1], accum=rs[:, i:i + 1], sig=b.sem)
                d = dve.wait(a).do(lambda e, i=i, rs=rs: e.reciprocal(rs[:, i:i + 1], rs[:, i:i + 1]), "row_rec")
                d = dve.wait(d).ts(t.ap[:, 0:n], t.ap[:, 0:n], rs[:, i:i + 1], None, ALU.mult, sig="probs")
                st[("P", h, i)] = (t, d)
            st[("S", h)] = mark

        def turn(h):
            values = self.freed(pt)
            for i in range(4):
                t, d = st[("P", h, i)]
                sl = slice(128 * i, 128 * i + 128)
                hi, lo = [pt.ap[:, 2048 * p:2048 * p + 2048].rearrange("p (j c) -> p j c", c=512)[:, 0:i + 1, sl]
                          for p in range(2)]
                st["T"] = self.turn_tile(t, d, i, ptr.next(), hi, lo, values)

        def values(h):
            v, vw = st[h]["v"]
            b = ob.next()
            c = 128 * (h % 2)
            pe.wait(st["T"], vw, self.freed(b))
            for j in range(4):
                vh = v[:, 256 * j + c:256 * j + c + 128]
                vl = v[:, 1024 + 256 * j + c:1152 + 256 * j + c]
                ph, pl = pt.ap[:, 640 * j:512 * j + 512], pt.ap[:, 2048 + 640 * j:2560 + 512 * j]
                mark = self.group(b.ap[:, 128 * j:512], [(vh, ph), (vl, ph), (vh, pl)], j == 0, j == 3,
                                  "pt" if j == 3 else None)
            t = self.tmp.next()
            d = dve.wait(mark, gw[h], self.freed(t)).stt(t.ap, b.ap, 0.5, gate[h], ALU.mult, ALU.mult, sig=b.sem)
            zw[h] = self.split(Z[:, 512 * h:512 * h + 512], Z[:, 4096 + 512 * h:4608 + 512 * h], t.ap, d, xg_read,
                               sig=t.sem)
            self.gate_read = d

        project(0)
        scores(0)
        for h in range(8):
            if h < 7:
                project(h + 1)
            turn(h)
            if h < 7:
                scores(h + 1)
            values(h)
        self.tmp = every
        self.out_proj("w_out_b", 8, lambda p, k: Z[:, 4096 * p + 512 * k:4096 * p + 512 * k + 512], zw,
                      [self.gate_read])

    def turn_tile(self, t, d, i, b, hi, lo, reuse):
        n = 128 * (i + 1)
        self.pe.wait(d, self.freed(b))
        for j in range(i + 1):
            mark = self.pe.turn(b.ap[:, 128 * j:128 * j + 128], t.ap[:, 128 * j:128 * j + 128], self.ident[:, :],
                                sig=t.sem if j == i else None)
        src = b.ap[:, 0:n]
        if len(hi.shape) == 3:
            src = src.rearrange("p (j c) -> p j c", c=128)
        a = self.act.wait(mark, reuse).act(hi, src, sig="pt_hi")
        return self.dve.wait(a).tt(lo, src, hi.bitcast(F32), ALU.subtract, sig=b.sem)

    def conv(self, u, uw, out, w3, sig):
        a = self.act.wait(uw, self.freed(out)).act(out.ap, u, scale=w3[2], sig="tap")
        b = self.dve.wait(a).stt(out.ap[:, 1:512], u[:, 0:511], w3[1], out.ap[:, 1:512], ALU.mult, ALU.add, sig="tap1")
        return self.dve.wait(b).stt(out.ap[:, 2:512], u[:, 0:510], w3[0], out.ap[:, 2:512], ALU.mult, ALU.add,
                                    sig=sig)

    def mixer(self, residual):
        FR, dve = self.FR, self.dve
        E = FR[:, 8192:16384]
        pr = Ring(self.bank[0:6])
        ew = {}
        for m in range(8):
            banks = [pr.next() for _ in range(3)]
            if m == 0:
                marks = self.proj_wide("w_sc_in_2", [8, 16, 0], KD, self.xin, banks,
                                       self.into(residual, "g_pre_mix_2", 0, self.y_last))
                y, yw, R, rw = self.stats(self.sq_mark, 1024, self.R)
                R2 = self.R2[:, :]
                r2 = dve.wait(rw).tt(R2, R, R, ALU.mult, sig="r_squared")
            else:
                marks = [self.proj("w_sc_in_2", 8 * (i + 1) % 24 + m, KD, self.xin, banks[i]) for i in range(3)]
            a, c, o = self.tmp.next(), self.tmp.next(), self.tmp.next()
            x = dve.wait(marks[0], r2, self.freed(a)).tt(a.ap, banks[0].ap, R2, ALU.mult, sig=banks[0].sem)
            x = dve.wait(marks[1], x, self.freed(c)).tt(c.ap, banks[1].ap, a.ap, ALU.mult, sig=banks[1].sem)
            v = self.conv(c.ap, x, o, [self.col("w_sc_conv_2", 8 * t + m) for t in range(3)], c.sem)
            x = dve.wait(marks[2], v).tt(a.ap, banks[2].ap, R, ALU.mult, sig=banks[2].sem)
            x = dve.wait(x).tt(a.ap, a.ap, o.ap, ALU.mult, sig=o.sem)
            ew[m] = self.split(E[:, 512 * m:512 * m + 512], E[:, 4096 + 512 * m:4608 + 512 * m], a.ap, x, sig=a.sem)
            if m == 3:
                self.bias_table()
        self.out_proj("w_sc_out_2", 8, lambda p, k: E[:, 4096 * p + 512 * k:4096 * p + 512 * k + 512], ew,
                      [self.y_read])

    def ffn(self, L, residual):
        FR, dve, act = self.FR, self.dve, self.act
        M = FR[:, 8192:8192 + 2 * NF * 512]
        pr = Ring(self.bank[0:6])
        name = f"w_ffn_up_2_{L}"
        mw = {}

        def taps(ch):
            return [self.col("w_ffn_conv_2", L * 132 + t * 44 + ch) for t in range(3)]

        def pair_out(m, banks, marks):
            outs = []
            for i in range(2):
                u, o = self.tmp.next(), self.tmp.next()
                x = dve.wait(marks[i], rw, self.freed(u)).tt(u.ap, banks[i].ap, R, ALU.mult, sig=banks[i].sem)
                outs.append((o, self.conv(u.ap, x, o, taps(m + NF * i), u.sem)))
            (c0, v0), (c1, v1) = outs
            t = self.tmp.next()
            a = act.wait(v0, self.freed(t)).act(t.ap, c0.ap, scale=0.5, func=ACT.Tanh, sig="tanh")
            x = dve.wait(a).stt(t.ap, t.ap, 1.0, c0.ap, ALU.add, ALU.mult, sig=c0.sem)
            x = dve.wait(x, v1).stt(t.ap, t.ap, 0.5, c1.ap, ALU.mult, ALU.mult, sig=c1.sem)
            mw[m] = self.split(M[:, 512 * m:512 * m + 512], M[:, (NF + m) * 512:(NF + m) * 512 + 512], t.ap, x,
                               self.y_last if m == 0 else None, sig=t.sem)

        banks = [pr.next() for _ in range(4)]
        marks = self.proj_wide(name, [0, NF, 1, NF + 1], KD, self.xin, banks,
                               self.into(residual, "g_pre_ffn_2", 8 * L, self.y_last))
        y, yw, R, rw = self.stats(self.sq_mark, 1024, self.R)
        pair_out(0, banks[0:2], marks[0:2])
        pair_out(1, banks[2:4], marks[2:4])
        for m in range(2, NF):
            banks = [pr.next(), pr.next()]
            marks = [self.proj(name, m, KD, self.xin, banks[0]), self.proj(name, NF + m, KD, self.xin, banks[1])]
            pair_out(m, banks, marks)
        self.out_proj(f"w_ffn_down_2_{L}", NF, lambda p, k: M[:, (NF * p + k) * 512:(NF * p + k) * 512 + 512], mw,
                      [self.y_read])

    def ple(self, L):
        FR, dve, act, sp = self.FR, self.dve, self.act, self.sp
        PT = FR[:, 8192:10240]
        pw = []
        for k in range(2):
            t = self.tmp.next()
            ld = sp.wait(self.freed(t)).dma(t.ap, self.ins["pT"][256 * L + 128 * k:256 * L + 128 * k + 128, :], f"p{k}")
            pw.append(self.split(PT[:, 512 * k:512 * k + 512], PT[:, 1024 + 512 * k:1536 + 512 * k], t.ap, ld,
                                 self.y_last, eng=dve, sig=t.sem))

        def pin(p, k):
            return PT[:, 1024 * p + 512 * k:1024 * p + 512 * k + 512]

        pr = Ring(self.bank[0:6])
        proj = {}

        def project(m):
            proj[m] = (b := pr.next(), self.proj(f"w_ple_proj_2_{L}", m, 2, pin, b, pw if m == 0 else None))

        residual = self.normed(1024, "g_post_ffn_2", 8 * L, 1.0, [lambda m=m: project(m) for m in range(3)])
        wide = [pr.next() for _ in range(3)]
        marks = self.proj_wide(f"w_ple_gate_2_{L}", [0, 1, 2], KD, self.xin, wide,
                               self.into(residual, "g_pre_ple_2", 8 * L, None))
        y, yw, R, rw = self.stats(self.sq_mark, 1024, self.R)
        for m in range(8):
            if m < 3:
                b0, r0 = wide[m], marks[m]
            else:
                project(m)
                b0 = pr.next()
                r0 = self.proj(f"w_ple_gate_2_{L}", m, KD, self.xin, b0)
            b1, r1 = proj[m]
            t = self.tmp.next()
            x = dve.wait(r0, rw, self.freed(t)).tt(t.ap, b0.ap, R, ALU.mult, sig=b0.sem)
            a = act.wait(x).act(t.ap, t.ap, scale=0.5, func=ACT.Tanh, sig="tanh")
            x = dve.wait(a, r1).stt(self.Y[m], t.ap, 1.0, b1.ap, ALU.add, ALU.mult, sig=b1.sem)
            if m < 7:
                self.acc_mark = self.square(m == 0, self.Y[m], x, t.sem)
            else:
                t7 = self.tmp.next()
                self.last_square = (t7, act.wait(x, self.freed(t7)).act(t7.ap, self.Y[m], func=ACT.Square, sig=t.sem))
            self.y_mark = x
        self.y_last = r0
        return self.normed(4096, "g_post_ple_2", 8 * L, 0.5)

    def bias_table(self):
        FD, sp, pe, act = self.FD, self.sp, self.pe, self.act
        scr = self.ins["scr"]
        oh, rb = FD[0:33, 4096:4736], FD[0:33, 4736:4744]
        sp.wait(self.gate_read).dma(rb, self.ins["rb"][:, :], "bias_in")
        ld = sp.dma(oh, self.ins["onehot"][:, :], "bias_in")
        slots, banks = [self.tmp.next(), self.tmp.next()], self.bank[6:8]
        pe.wait(ld)
        for h in range(8):
            for i in range(2):
                b, t = banks[i], slots[i]
                pe.wait(self.freed(b))
                m = pe.mm(b.ap[:, 0:320], rb[:, h:h + 1].broadcast_to([33, P]), oh[:, 320 * i:320 * i + 320],
                          True, True, sig="pe_bias")
                a = act.wait(m, self.freed(t)).act(t.ap[:, 0:320], b.ap[:, 0:320], scale=8.0, sig=b.sem)
                dst = bass.AP(scr.tensor, h * P * (TW + 1) + 320 * i, [[TW + 1, P], [1, 320]])
                sp.wait(a).dma(dst, t.ap[:, 0:320], t.sem)
        self.scrw = [self.freed(t) for t in slots]

    def diff(self, residual):
        FR, FD, dve, act, pe, sp = self.FR, self.FD, self.dve, self.act, self.pe, self.sp
        D0 = 8192
        KZ, V = FR[:, D0:D0 + 8192], FR[:, D0 + 8192:D0 + 16384]
        qb = Ring([Slot(FR[:, D0 + 16384 + 2048 * i:D0 + 18432 + 2048 * i], f"qb{i}") for i in range(2)])
        pt = Slot(FR[:, D0 + 20480:D0 + 23040], "pt")
        TB = FD[:, 0:4096].rearrange("p (h c) -> p h c", h=8)
        ONr = Ring([Slot(FD[:, 4096 + 512 * i:4608 + 512 * i], f"on{i}") for i in range(2)])
        lv = self.tmp.next()
        ld = sp.wait(self.freed(lv)).dma(lv.ap[:, 0:256], bass.AP(self.ins["lam"].tensor, 0, [[0, P], [1, 256]]),
                                         "lam")
        d2, e2, lam, gs = self.keep[:, 0:2], self.keep[:, 2:4], self.keep[:, 4:5], self.keep[:, 5:6]
        dve.wait(ld)
        for i in range(2):
            o = 128 * i
            x = dve.tt(lv.ap[:, 256 + 64 * i:320 + 64 * i], lv.ap[:, o:o + 64], lv.ap[:, o + 64:o + 128], ALU.mult,
                       sig="lam_dve")
        x = dve.wait(x).do(lambda e: e.tensor_reduce(d2, lv.ap[:, 256:384].rearrange("p (a b) -> p a b", a=2), AXX,
                                                     ALU.add), lv.sem)
        a = act.wait(x).act(e2, d2, func=ACT.Exp, sig="lam_act")
        x = dve.wait(a).tt(lam, e2[:, 1:2], e2[:, 0:1], ALU.subtract, sig="lam_dve")
        lamw = dve.wait(x).ts(lam, lam, -LAMBDA_INIT, None, ALU.add, sig="lam_dve")
        gsw = dve.ts(gs, self.col("g_subln_2", 0), 1.0 - LAMBDA_INIT, None, ALU.mult, sig="lam_dve")
        dve.wait(self.y_last)
        for b in qb.slots:
            for p in range(2):
                o = 1024 * p
                half = slice(64, 128) if p == 0 else slice(0, 64)
                zq = dve.do(lambda e, b=b, o=o, half=half: e.memset(b.ap[half, o:o + 1024].bitcast(F32), 0.0),
                            "zero_q")
        pr = Ring(self.bank[0:6])
        kw, vw = {}, {}
        wide = [pr.next() for _ in range(4)]
        marks = self.proj_wide("w_kv_2", [0, 1, 2, 3], KD, self.xin, wide,
                               self.into(residual, "g_kv_2", 0, self.y_last))
        src = bass.AP(self.ins["scr"].tensor, P - 1, [[TW, P], [P * (TW + 1), 8], [1, 512]])
        tbw = sp.wait(*self.scrw, self.y_read).dma(TB, src, "bias_table")
        y, yw, R, rw = self.stats(self.sq_mark, 1024, self.R)
        for h in range(8):
            if h < 4:
                b, mark = wide[h], marks[h]
            else:
                b = pr.next()
                mark = self.proj("w_kv_2", h, KD, self.xin, b)
            t = self.tmp.next()
            d = dve.wait(mark, rw, self.freed(t)).tt(t.ap, b.ap, R, ALU.mult, sig=b.sem)
            kw[h] = self.split(KZ[:, 1024 * h:1024 * h + 512], KZ[:, 1024 * h + 512:1024 * h + 1024], t.ap, d,
                               sig=t.sem)
        for c in range(4):
            outs = self.proj_nat("w_kv_2", [8 + 2 * c, 9 + 2 * c], KD, self.xin, pr)
            vw[c] = self.tokens_out(outs, y, yw, lambda t: (V[:, 1024 * t + 256 * c:1024 * t + 256 * c + 256],
                                                           V[:, 4096 + 1024 * t + 256 * c:4352 + 1024 * t + 256 * c]),
                                    None)
        xg_read = self.unit_end[(len(self.order) - 1) // UNIT]
        xq = [self.xg_tile("g_pre_mix_2", 8, k, None, xg_read if k == 0 else None) for k in range(KD)]
        pr, srg = Ring(self.bank[0:1]), Ring(self.bank[1:5])
        ptr, ob = Ring(self.bank[5:6]), Ring(self.bank[6:7])
        st, zw = {}, {}

        def project(h):
            b = pr.next()
            mark = self.proj("w_q_2", h, KD, self.xin, b, xq if h == 0 else None)
            t = self.tmp.next()
            d = dve.wait(mark, self.freed(t)).tt(t.ap, b.ap, R, ALU.mult, sig=b.sem)
            q = qb.next()
            act.wait(d, self.freed(q))
            for p in range(2):
                hs, o = slice(64 * p, 64 * p + 64), 1024 * p
                a = act.act(q.ap[hs, o:o + 512], t.ap[hs, :], sig="q_hi")
            w = kw[7]
            if h:
                w = st[h - 1][1]
            self.pool.wait(a)
            for p in range(2):
                hs, o = slice(64 * p, 64 * p + 64), 1024 * p
                w = self.pool.wait(w).tt(q.ap[hs, o + 512:o + 1024], t.ap[hs, :], q.ap[hs, o:o + 512].bitcast(F32),
                                         ALU.subtract, sig=t.sem if p else "q_lo")
            st[h] = (q, w)

        def scores(h, i):
            q, qw = st[h]
            n = 128 * (i + 1)
            mx, rs = self.small(2), self.small(2)
            Ps = []
            kh, kl = KZ[:, 1024 * h:1024 * h + n], KZ[:, 1024 * h + 512:1024 * h + 512 + n]
            if i == 0:
                pe.wait(qw, kw[h], zq)
                dve.wait(tbw)
            for p in range(2):
                b = srg.next()
                o = 1024 * p + 128 * i
                qh, ql = q.ap[:, o:o + 128], q.ap[:, o + 512:o + 640]
                pe.wait(self.freed(b))
                mark = self.group(b.ap[:, 0:n], [(qh, kh), (qh, kl), (ql, kh)],
                                  sig=q.sem if (i, p) == (3, 1) else "pe_scores")
                t = self.tmp.next()
                m = mx[:, p:p + 1]
                d = dve.wait(mark, self.freed(t)).do(
                    lambda e, t=t, b=b, m=m: e.tensor_tensor_reduce(t.ap[:, 0:n], b.ap[:, 0:n], TB[:, h, 512 - n:512],
                                                                    0.125, -3.0e38, ALU.add, ALU.max, m), b.sem)
                Ps.append((t, d))
            d = dve.wait(d).ts(mx, mx, -1.0, None, ALU.mult, sig="row_max")
            act.wait(d)
            for p in range(2):
                t = Ps[p][0]
                a = act.act(t.ap[:, 0:n], t.ap[:, 0:n], func=ACT.Exp, bias=mx[:, p:p + 1], accum=rs[:, p:p + 1],
                            sig="exp")
            (t0, _), (t1, _) = Ps
            d = dve.wait(a).do(lambda e: e.reciprocal(rs, rs), "row_rec")
            a = act.wait(d).act(t0.ap[:, 0:n], t0.ap[:, 0:n], scale=rs[:, 0:1], sig="probs0")
            d = dve.wait(lamw, d).tt(rs[:, 1:2], rs[:, 1:2], lam, ALU.mult, sig="row_rec")
            x = dve.wait(a, d).stt(t0.ap[:, 0:n], t1.ap[:, 0:n], rs[:, 1:2], t0.ap[:, 0:n], ALU.mult, ALU.add,
                                   sig=t1.sem)
            st[("P", h, i)] = (t0, x)
            st[("sl", h)] = mark

        def turn(h, i):
            t, d = st.pop(("P", h, i))
            o, n = self.pt_off(i), 128 * (i + 1)
            if i == 0:
                st["pt_free"] = self.freed(pt)
            st[("T", h)] = self.turn_tile(t, d, i, ptr.next(), pt.ap[:, o:o + n], pt.ap[:, 1280 + o:1280 + o + n],
                                          st["pt_free"])

        def values(h):
            b = ob.next()
            ss, rs = self.small(4), self.small(4)
            o4 = b.ap
            pe.wait(st[("T", h)], vw[h // 2], self.freed(b))
            for i in range(4):
                terms = []
                for j in range(i + 1):
                    o = self.pt_off(i) + 128 * j
                    ph, pl = pt.ap[:, o:o + 128], pt.ap[:, 1280 + o:1280 + o + 128]
                    c = 1024 * j + 128 * h
                    vh, vl = V[:, c:c + 128], V[:, 4096 + c:4224 + c]
                    terms += [(ph, vh), (pl, vh), (ph, vl)]
                mark = self.group(o4[:, 128 * i:128 * i + 128], terms, sig=pt.sem if i == 3 else None)
            t = self.tmp.next()
            act.wait(mark, self.freed(t))
            for i in range(4):
                a = act.act(t.ap[:, 128 * i:128 * i + 128], o4[:, 128 * i:128 * i + 128], func=ACT.Square,
                            accum=ss[:, i:i + 1], sig=t.sem if i == 3 else None)
            d = dve.wait(a).ts(ss, ss, 1.0 / 128, EPS, ALU.mult, ALU.add, sig="o_var")
            d = self.newton(ss, rs, d)
            on = ONr.next()
            dve.wait(d, self.freed(on))
            for i in range(4):
                x = dve.ts(on.ap[:, 128 * i:128 * i + 128], o4[:, 128 * i:128 * i + 128], rs[:, i:i + 1], None,
                           ALU.mult, sig=b.sem if i == 3 else None)
            st[("O", h)] = (on, x)

        def finish(h):
            on, x = st[("O", h)]
            b = self.bank[7]
            pe.wait(x, self.freed(b))
            for i in range(4):
                mark = pe.turn(b.ap[:, 128 * i:128 * i + 128], on.ap[:, 128 * i:128 * i + 128], self.ident[:, :],
                               sig=on.sem if i == 3 else None)
            hi, lo = KZ[:, 1024 * h:1024 * h + 512], KZ[:, 1024 * h + 512:1024 * h + 1024]
            a = act.wait(mark, gsw, st[("sl", h)]).act(hi, b.ap, scale=gs, sig="z_hi")
            zw[h] = dve.wait(a).stt(lo, b.ap, gs, hi.bitcast(F32), ALU.mult, ALU.subtract, sig=b.sem)

        project(0)
        for h in range(8):
            for i in range(4):
                scores(h, i)
                if i == 1 and h:
                    values(h - 1)
                if i == 3 and h:
                    finish(h - 1)
                if i >= 1:
                    turn(h, i - 1)
                if i == 2 and h < 7:
                    project(h + 1)
            turn(h, 3)
        values(7)
        finish(7)
        self.out_proj("w_o_2", 8, lambda p, k: KZ[:, 1024 * k + 512 * p:1024 * k + 512 * p + 512], zw,
                      [zw[7], st[("O", 7)][1]])

    def pt_off(self, i):
        return [0, 128, 384, 768][i]

    def build(self):
        sp, dve = self.sp, self.dve
        self.cold = sp.dma(self.cols[:, :], self.ins["cols"][:, :], "cols")
        xw = []
        for k in range(KD):
            xw.append(sp.dma(self.xt(k), self.ins["xT"][P * k:P * k + P, :], f"x{k}"))
            if k == 1:
                self.stream_start()
        sp.dma(self.ident[:, :], self.ins["ident"][:, :], "consts")
        consts = sp.dma(self.masks[:, :], self.ins["masks"][:, :], "consts")
        one = dve.do(lambda e: e.memset(self.ones[:, :], 1.0), "ones")
        self.act.wait(self.cold, consts)
        dve.wait(self.cold, consts)
        self.retention(xw)
        self.latent(self.normed(1024, "g_post_a", 0))
        while len(self.order) % UNIT:
            self.order.append(None)
        self.mixer(self.normed(1024, "g_post_b", 0))
        self.ffn(0, self.normed(1024, "g_post_mix_2", 0))
        residual = self.ple(0)
        self.diff(residual)
        self.ffn(1, self.normed(1024, "g_post_mix_2", 8))
        residual = self.ple(1)
        for k in range(KD):
            done = sp.wait(residual(k)).dma(self.out[P * k:P * k + P, :], self.xt(k), "out")
        sp.wait(done).do(lambda e: e.nop())
        assert -(-len(self.order) // UNIT) == self.NU, len(self.order)

    def emit(self):
        nc, ctx = self.nc, self.ctx
        sems = {n: ctx.enter_context(nc.semaphore("s_" + n)) for n in self.counts}
        block = ctx.enter_context(nc.Block())

        @block.sync
        def _(e):
            self.sp.issue(e, sems)

        @block.scalar
        def _(e):
            self.act.issue(e, sems)

        @block.vector
        def _(e):
            self.dve.issue(e, sems)

        @block.gpsimd
        def _(e):
            self.pool.issue(e, sems)

        @block.tensor
        def _(e):
            self.pe.issue(e, sems)


NUNITS = 311


def build_program(nc, ins, out):
    from contextlib import ExitStack

    with ExitStack() as ctx:
        p = Net(nc, ctx, ins, out)
        p.build()
        p.emit()
    return p.order


def shape_constants():
    f = np.float32
    heads = np.arange(8, dtype=np.float64)
    lg = np.log(1.0 - np.exp2(-5.0 - heads))
    k, q = np.arange(128)[:, None], np.arange(512)[None, :]
    ok = (k // 64) <= (q // 64)
    dec = np.exp(lg[:, None, None] * np.abs(q - k)[None]) * ok[None] * 128.0 ** -0.5
    out = {"decay": dec.reshape(8 * 128, 512).astype(f)}
    pos = np.arange(512, dtype=f)

    def angles(half):
        inv = (f(10000.0) ** (-np.arange(half, dtype=f) / f(half))).astype(f)
        return (pos[:, None] * inv[None, :]).astype(f).astype(np.float64).T

    for name, half in (("rope_a", 64), ("rope_b", 32)):
        a = angles(half)
        i = np.arange(128) % half
        c, s = np.cos(a)[i], np.sin(a)[i]
        s = np.where(np.arange(128)[:, None] < 64, s, -s)
        out[name] = np.concatenate([c, s], axis=1).astype(f)
    out["ident"] = np.eye(128, dtype=f)
    qq, kk = np.arange(128)[:, None], np.arange(128)[None, :]
    out["mask"] = np.where(kk // 64 <= qq // 64, 0.0, NEG).astype(f)
    par = (np.arange(128) // 32) % 2
    out["masks"] = np.stack([par == 0, par == 1], axis=1).astype(f)
    dist = 511 - np.arange(TW)
    d = np.maximum(dist, 1).astype(f)
    large = 16 + (np.log(d / f(16)).astype(f) / f(math.log(128 / 16)) * f(16)).astype(np.int32)
    bucket = np.where(dist < 16, dist, np.minimum(large, 31))
    oh = np.zeros((33, TW), f)
    for e in range(TW):
        if dist[e] >= 0:
            oh[bucket[e], e] = 1.0
        else:
            oh[32, e] = 1.0
    out["onehot"] = oh
    return out


def lay_out(inputs, order):
    f = np.float32
    a = {n: np.asarray(v) for n, v in inputs.items()}
    w = {"w_in_a": a["w_in_a"][0], "w_out_a": a["w_out_a"][0], "w_kv_a": a["w_kv_a"], "w_uk": a["w_uk"],
         "w_uv": a["w_uv"], "w_in_b": a["w_in_b"][0], "w_uq": a["w_uq"][0], "w_out_b": a["w_out_b"][0],
         "w_sc_in_2": a["w_sc_in_2"][0], "w_sc_out_2": a["w_sc_out_2"][0], "w_kv_2": a["w_kv_2"],
         "w_q_2": a["w_q_2"][0], "w_o_2": a["w_o_2"][0]}
    for n in ("w_ffn_up_2", "w_ffn_down_2", "w_ple_gate_2", "w_ple_proj_2"):
        for L in range(2):
            w[f"{n}_{L}"] = a[n][L]
    ws = np.zeros((NUNITS, 128, UNIT, 128), f)
    for i, block in enumerate(order):
        if block is None:
            continue
        name, k, cols = block
        m = w[name][128 * k:128 * k + 128]
        ws[i // UNIT, :, i % UNIT, :] = m[:, 128 * cols:128 * cols + 128] if isinstance(cols, int) else m[:, cols]
    out = {"ws": ws.reshape(-1, 128 * UNIT)}
    cols = np.zeros((128, NCOL), f)
    for n, at in COLS.items():
        v = a[n].reshape(-1, 128).T
        cols[:, at:at + v.shape[1]] = v
    out["cols"] = cols
    out["xT"] = np.ascontiguousarray(a["x"][0].T)
    out["pT"] = np.ascontiguousarray(a["p_2"][:, 0].transpose(0, 2, 1).reshape(512, 512))
    rb = np.full((33, 8), NEG, f)
    rb[0:32] = a["rel_bias_2"]
    out["rb"] = rb
    out["lam"] = np.ascontiguousarray(a["diff_lambda_2"].reshape(1, 256))
    return out


def kernel(**inputs):
    import concourse.bacc as _bacc
    from concourse.bass_utils import run_bass_kernel_spmd as _run

    nc = _bacc.Bacc("TRN2", target_bir_lowering=False, num_devices=1, dynamic_dma_scratch_size=256)
    consts = shape_constants()
    shapes = {n: v.shape for n, v in consts.items()}
    shapes.update(ws=(NUNITS * 128, 128 * UNIT), cols=(128, NCOL), xT=(1024, 512), pT=(512, 512), rb=(33, 8),
                  lam=(1, 256))
    ins = {n: nc.dram_tensor("in_" + n, s, F32, kind="ExternalInput").ap() for n, s in shapes.items()}
    ins["scr"] = nc.dram_tensor("scr", (8, 128 * (TW + 1)), F32).ap()
    out = nc.dram_tensor("out_0_dram", (1024, 512), F32, kind="ExternalOutput").ap()
    order = build_program(nc, ins, out)
    arrays = lay_out(inputs, order)
    arrays.update(consts)
    r = _run(nc, [{"in_" + n: v for n, v in arrays.items()}], core_ids=[0])
    got = r.results[0]["out_0_dram"]
    return np.ascontiguousarray(got.T).reshape(1, 512, 1024)
```

```python
import math

import numpy as np

import concourse.bass as bass
from concourse import mybir

F32 = mybir.dt.float32
F32R = mybir.dt.float32r
I32 = mybir.dt.int32
ALU = mybir.AluOpType
ACT = mybir.ActivationFunctionType
AXX = mybir.AxisListType.X

P = 128
S = 512
KD = 8
EPS = 1e-6
UNIT = 8
RING = 4
AHEAD = 2
STAGES = 3
NF = 22
MAGIC = float(0x5F3759DF)
LAMBDA_INIT = 0.8 - 0.6 * math.exp(-0.3)
NEG = -1.0e30
TW = 640

COLS = {}
_at = 0
for _name, _n in (("g_pre_a", 8), ("gn_gain_a", 16), ("g_post_a", 8), ("g_kv", 8), ("g_kv_lat", 2), ("g_pre_b", 8),
                  ("g_q_lat", 3), ("g_post_b", 8), ("g_pre_mix_2", 16), ("g_post_mix_2", 16), ("g_pre_ffn_2", 16),
                  ("g_post_ffn_2", 16), ("g_pre_ple_2", 16), ("g_post_ple_2", 16), ("w_sc_conv_2", 24),
                  ("g_kv_2", 8), ("g_subln_2", 1), ("w_ffn_conv_2", 264)):
    COLS[_name] = _at
    _at += _n
NCOL = _at


class Slot:

    def __init__(self, ap, sem):
        self.ap, self.sem = ap, sem


class Ring:
    def __init__(self, slots):
        self.slots, self.n = slots, 0

    def next(self):
        b = self.slots[self.n % len(self.slots)]
        self.n += 1
        return b


class Engine:

    def __init__(self, counts):
        self.steps, self.counts = [], counts

    def wait(self, *marks):
        self.steps += [(None, m[0], m[1]) for m in marks if m is not None and m[1] > 0]
        return self

    def do(self, fn, sig=None, inc=1):
        if sig is not None:
            self.counts[sig] = self.counts.get(sig, 0) + inc
        self.steps.append((fn, sig, inc))
        return sig, self.counts.get(sig, 0)

    def dma(self, out, in_, sig):
        return self.do(lambda e: e.dma_start(out, in_), sig, 16)

    def act(self, out, in_, scale=1.0, func=ACT.Copy, bias=0.0, accum=None, sig=None):
        if accum is None:
            return self.do(lambda e: e.activation(out, in_, func, bias=bias, scale=scale), sig)
        return self.do(lambda e: e.activation(out, in_, func, bias=bias, scale=scale, accum_out=accum), sig)

    def tt(self, out, a, b, op, sig=None):
        return self.do(lambda e: e.tensor_tensor(out, a, b, op), sig)

    def stt(self, out, a, s, b, op0, op1, sig=None):
        return self.do(lambda e: e.scalar_tensor_tensor(out=out, in0=a, scalar=s, in1=b, op0=op0, op1=op1), sig)

    def ts(self, out, a, s1, s2, op0, op1=None, sig=None):
        if s2 is None:
            return self.do(lambda e: e.tensor_scalar(out, a, s1, None, op0), sig)
        return self.do(lambda e: e.tensor_scalar(out, a, s1, s2, op0, op1), sig)

    def mm(self, out, lhsT, rhs, start, stop, sig=None):
        return self.do(lambda e: e.matmul(out, lhsT, rhs, start=start, stop=stop), sig)

    def turn(self, out, in_, ident, sig=None):
        return self.do(lambda e: e.transpose(out, in_, ident), sig)

    def issue(self, e, sems):
        for fn, sig, n in self.steps:
            if fn is None:
                e.wait_ge(sems[sig], n)
            else:
                ins = fn(e)
                if sig is not None:
                    ins.then_inc(sems[sig], n)


class Net:
    def __init__(self, nc, ctx, ins, out):
        self.nc, self.ctx, self.ins, self.out = nc, ctx, ins, out
        self.counts = {}
        self.pe, self.act, self.dve, self.pool, self.sp = (Engine(self.counts) for _ in range(5))
        self.order = []
        self.NU = ins["ws"].shape[0] // P
        self.alloc()

    def alloc(self):
        nc, ctx = self.nc, self.ctx

        def sb(name, n, dt):
            return ctx.enter_context(nc.sbuf_tensor(name, [P, n], dt))

        self.WH = sb("WH", RING * 1024, F32R)
        self.WL = sb("WL", RING * 1024, F32R)
        self.stage = sb("stage", STAGES * 1024, F32)
        self.FR = sb("FR", 8192 + 23040, F32R)
        self.MK = self.FR[:, 8192 + 22528:8192 + 22784]
        self.X = sb("X", 4096, F32)
        self.R = sb("R", 512, F32)
        self.R2 = sb("R2", 512, F32)
        self.T = sb("T", 6 * 512, F32)
        self.FD = sb("FD", 5120, F32)
        self.cols = sb("cols", NCOL, F32)
        self.ident = sb("ident", 128, F32)
        self.ones = sb("ones", 2, F32)
        self.sm = sb("sm", 160, F32)
        self.held = sb("held", 72, F32)
        self.keep = sb("keep", 24, F32)
        self.masks = sb("masks", 2, F32)
        self.acc = sb("acc", 512, F32)
        self.bank = [Slot(ctx.enter_context(nc.psum_tensor(f"pb{i}", [P, 512], F32))[:, :], f"bank{i}")
                     for i in range(8)]
        self.tmp = Ring([Slot(self.T[:, 512 * i:512 * i + 512], f"tmp{i}") for i in range(6)])
        self.smn = self.nheld = 0
        self.Y = [self.FD[:, 512 * m:512 * m + 512] for m in range(8)]
        self.y_slots = [Slot(y, f"y{m}") for m, y in enumerate(self.Y)]

    def small(self, n):
        if self.smn + n > 160:
            self.smn = 0
        a = self.sm[:, self.smn:self.smn + n]
        self.smn += n
        return a

    def xt(self, k):
        return self.X[:, 512 * k:512 * k + 512]

    def xin(self, part, k):
        return self.FR[:, part * 4096 + 512 * k:part * 4096 + 512 * k + 512]

    def col(self, name, i):
        c = COLS[name] + i
        return self.cols[:, c:c + 1]

    def count(self, sem):
        return sem, self.counts.get(sem, 0)

    def freed(self, slot):
        return self.count(slot.sem)

    def stream_start(self):
        self.loads = self.splits = 0
        self.loaded, self.unit_ready, self.unit_end, self.pe_at = [], [], {}, -1

    def load_unit(self):
        u = self.loads
        if u >= self.NU:
            return
        self.loads += 1
        s = u % STAGES
        if u >= STAGES:
            self.sp.wait(self.unit_ready[u - STAGES])
        self.loaded.append(self.sp.dma(self.stage[:, 1024 * s:1024 * s + 1024], self.ins["ws"][P * u:P * u + P, :],
                                       f"load{s}"))

    def split_unit(self):
        u = self.splits
        self.splits += 1
        s, w = u % STAGES, u % RING
        src = self.stage[:, 1024 * s:1024 * s + 1024]
        hi, lo = self.WH[:, 1024 * w:1024 * w + 1024], self.WL[:, 1024 * w:1024 * w + 1024]
        used = self.unit_end[u - RING] if u >= RING else None
        a = self.act.wait(self.loaded[u], used).act(hi, src, sig="w_hi")
        self.unit_ready.append(self.dve.wait(a).tt(lo, src, hi.bitcast(F32), ALU.subtract, sig="w_lo"))
        self.load_unit()

    def blocks(self, specs):
        at = len(self.order)
        self.order += specs
        u, o = at // UNIT, 128 * (at % UNIT)
        n = 128 * len(specs)
        assert o + n <= 128 * UNIT
        while self.splits <= min(u + AHEAD, self.NU - 1):
            self.split_unit()
        w = 1024 * (u % RING) + o
        return self.WH[:, w:w + n], self.WL[:, w:w + n], u

    def pe_unit(self, u):
        if u > self.pe_at:
            self.pe.wait(self.unit_ready[u])
            self.pe_at = u

    def group(self, out, terms, first=True, last=True, sig=None):
        n = len(terms)
        for i, (l, r) in enumerate(terms):
            mark = self.pe.mm(out, l, r, first and i == 0, last and i == n - 1, sig if i == n - 1 else None)
        return mark

    def proj(self, name, cols, K, xin, bank, ready=None):
        self.pe.wait(self.freed(bank))
        for k in range(K):
            wh, wl, u = self.blocks([(name, k, cols)])
            self.pe_unit(u)
            if ready:
                self.pe.wait(ready[k])
            mark = self.group(bank.ap, [(wh, xin(0, k)), (wh, xin(1, k)), (wl, xin(0, k))], k == 0, k == K - 1,
                              "pe_proj")
            self.unit_end[u] = mark
        return mark

    def proj_wide(self, sets, banks, prepare, K=KD, between=None):
        marks = [None] * len(sets)
        ahead = [prepare(0)]
        for k in range(K):
            if k + 1 < K:
                ahead.append(prepare(k + 1))
            for n, (name, cols, xin) in enumerate(sets):
                if k == 0:
                    self.pe.wait(self.freed(banks[n]))
                wh, wl, u = self.blocks([(name, k, cols)])
                self.pe_unit(u)
                if n == 0:
                    self.pe.wait(ahead[k])
                marks[n] = self.group(banks[n].ap, [(wh, xin(0, k)), (wh, xin(1, k)), (wl, xin(0, k))],
                                      k == 0, k == K - 1, "pe_proj")
                self.unit_end[u] = marks[n]
            if between and k in between:
                between[k]()
        return marks

    def entry(self, sets, banks, prepare, D=1024, at=5):
        s = {}

        def sums():
            s["y"] = self.rms(self.token_sums(self.acc_mark), D)

        def over():
            m = self.spread(*s["y"])
            s["r"] = self.act.wait(m).act(self.R[:, :], self.bank[6].ap, sig=self.bank[6].sem)

        marks = self.proj_wide(sets, banks, prepare, KD, {at: sums, at + 1: over})
        return marks, s["y"][0], s["y"][1], self.R[:, :], s["r"]

    def proj_nat(self, name, wide, K, xin, ring, ready=None):
        bl = [self.blocks([(name, k, c) for c in wide]) for k in range(K)]
        outs = []
        for p in range(2):
            bank = ring.next()
            self.pe.wait(self.freed(bank))
            for t in (2 * p, 2 * p + 1):
                sl = slice(128 * t, 128 * t + 128)
                ap = bank.ap[:, 256 * (t % 2):256 * (t % 2) + 256]
                for k in range(K):
                    wh, wl, u = bl[k]
                    self.pe_unit(u)
                    if ready:
                        self.pe.wait(ready[k])
                    mark = self.group(ap, [(xin(0, k)[:, sl], wh), (xin(0, k)[:, sl], wl), (xin(1, k)[:, sl], wh)],
                                      k == 0, k == K - 1, "pe_proj")
                    self.unit_end[u] = mark
            outs.append((bank, mark))
        return outs

    def tokens_out(self, outs, y, yw, dst, reuse):
        for p, (bank, mark) in enumerate(outs):
            self.act.wait(mark, yw, reuse)
            for t in (2 * p, 2 * p + 1):
                a = self.act.act(dst(t)[0], bank.ap[:, 256 * (t % 2):256 * (t % 2) + 256], scale=y[:, t:t + 1],
                                 sig="tok_hi")
            self.dve.wait(a)
            for t in (2 * p, 2 * p + 1):
                hi, lo = dst(t)
                d = self.dve.stt(lo, bank.ap[:, 256 * (t % 2):256 * (t % 2) + 256], y[:, t:t + 1], hi.bitcast(F32),
                                 ALU.mult, ALU.subtract, sig=bank.sem if t % 2 else None)
        return d

    def newton(self, a, y, after, out_scale=1.0):
        dve = self.dve
        t = self.small(a.shape[-1])
        c = 0.375 * out_scale
        m = dve.wait(after).ts(t.bitcast(I32), a.bitcast(I32), 1, None, ALU.logical_shift_right, sig="newton")
        m = dve.wait(m).ts(y.bitcast(I32), t.bitcast(I32), -1.0, MAGIC, ALU.mult, ALU.add, sig="newton")
        m = dve.wait(m).stt(t, y, -0.5 * c, y, ALU.mult, ALU.mult, sig="newton")
        m = dve.wait(m).tt(t, t, a, ALU.mult, sig="newton")
        m = dve.wait(m).stt(y, t, 1.5 * c, y, ALU.add, ALU.mult, sig="newton")
        m = dve.wait(m).stt(t, y, 1.0 / (c * c), y, ALU.mult, ALU.mult, sig="newton")
        m = dve.wait(m).tt(t, t, a, ALU.mult, sig="newton")
        m = dve.wait(m).stt(t, t, -10.0 / 3.0, t, ALU.add, ALU.mult, sig="newton")
        return dve.wait(m).stt(y, t, 5.0, y, ALU.add, ALU.mult, sig="newton")

    def square(self, first, src, after, sig="sq"):
        if first:
            self.acc_mark = self.act.wait(after).act(self.acc[:, :], src, func=ACT.Square, sig=sig)
            return self.acc_mark
        t = self.tmp.next()
        a = self.act.wait(after, self.freed(t)).act(t.ap, src, func=ACT.Square, sig=sig)
        self.acc_mark = self.pool.wait(a, self.acc_mark).tt(self.acc[:, :], self.acc[:, :], t.ap, ALU.add, sig=t.sem)
        return self.acc_mark

    def token_sums(self, after, more=None):
        b = self.bank[7]
        self.pe.wait(after, self.freed(b))
        for c in range(4):
            sl = slice(128 * c, 128 * c + 128)
            m = self.pe.mm(b.ap[:, c:c + 1], self.acc[:, sl], self.ones[:, 0:1], True, more is None, sig="pe_sums")
            if more is not None:
                if c == 0:
                    self.pe.wait(more[1])
                m = self.pe.mm(b.ap[:, c:c + 1], more[0].ap[:, sl], self.ones[:, 0:1], False, True,
                               sig=more[0].sem if c == 3 else "pe_sums")
        return m

    def rms(self, sums, D, out_scale=1.0):
        a, y = self.small(4), self.held[:, self.nheld:self.nheld + 4]
        self.nheld += 4
        m = self.dve.wait(sums).ts(a, self.bank[7].ap[:, 0:4], 1.0 / D, EPS, ALU.mult, ALU.add, sig=self.bank[7].sem)
        return y, self.newton(a, y, m, out_scale)

    def spread(self, y, yw):
        b = self.bank[6]
        self.pe.wait(yw, self.freed(b))
        for c in range(4):
            m = self.pe.mm(b.ap[:, 128 * c:128 * c + 128], y[:, c:c + 1].broadcast_to([P, P]), self.ident[:, :],
                           True, True, sig="pe_spread")
        return m

    def xg_tile(self, name, base, k, after, reuse=None):
        return self.xg_lo(self.xg_hi(name, base, k, after, reuse))

    def xg_hi(self, name, base, k, after, reuse=None, at=0):
        g = self.col(name, base + k)
        hi, lo = [self.FR[:, at + part * 4096 + 512 * k:at + part * 4096 + 512 * k + 512] for part in range(2)]
        a = self.act.wait(after, reuse).act(hi, self.xt(k), scale=g, sig="xg_hi")
        return k, g, hi, lo, a

    def xg_lo(self, half):
        k, g, hi, lo, a = half
        return self.dve.wait(a).stt(lo, self.xt(k), g, hi.bitcast(F32), ALU.mult, ALU.subtract, sig="xg_lo")

    def out_tile(self, m, mark, bank, more=None):
        if m == 0:
            self.acc_mark = self.act.wait(mark).act(self.acc[:, :], bank.ap, func=ACT.Square, sig="sq")
        else:
            t = self.tmp.next()
            a = self.act.wait(mark, self.freed(t)).act(t.ap, bank.ap, func=ACT.Square, sig="sq")
            if m < 7:
                self.acc_mark = self.pool.wait(a, self.acc_mark).tt(self.acc[:, :], self.acc[:, :], t.ap, ALU.add, sig=t.sem)
            else:
                self.last_square = (t, a)
        self.y_mark = self.act.act(self.Y[m], bank.ap, sig=bank.sem)

    def out_proj(self, name, K, xin, ready, reuse, ring=None, between=None):
        ring = ring or Ring(self.bank[0:6])
        wide = [ring.next() for _ in range(4)]
        marks = self.proj_wide([(name, m, xin) for m in range(4)], wide, lambda k: ready[k], K, between)
        self.act.wait(*reuse())
        for m in range(8):
            if m < 4:
                b, mark = wide[m], marks[m]
            else:
                b = ring.next()
                mark = self.proj(name, m, K, xin, b)
            self.out_tile(m, mark, b)
        self.y_last = mark

    def normed(self, D, gname, gbase, out_scale=1.0, filler=()):
        filler = list(filler)
        if filler:
            filler.pop(0)()
        sums = self.token_sums(self.acc_mark, self.last_square)
        y, yw = self.rms(sums, D, out_scale)
        for f in filler:
            f()
        m = self.spread(y, yw)

        def scaled(k):
            t = self.tmp.next()
            if k == 0:
                self.dve.wait(m, self.y_mark)
            self.y_read = self.dve.wait(self.freed(t)).stt(t.ap, self.Y[k], self.col(gname, gbase + k),
                                                           self.bank[6].ap, ALU.mult, ALU.mult,
                                                           sig=self.bank[6].sem if k == 7 else "y_normed")
            return t, self.y_read

        def added(k, t, after):
            return self.dve.wait(after).tt(self.xt(k), self.xt(k), t.ap, ALU.add, sig=t.sem)

        return scaled, added

    def into(self, residual, gains, reuse):
        scaled, added = residual
        ts, halves = {}, {}

        def add(k):
            x = added(k, *ts[k])
            halves[k] = [self.xg_hi(name, base, k, x, reuse if k == 0 else None, at) for name, base, at in gains]
            self.square(k == 0, self.xt(k), x)

        def prepare(k):
            if k == 0:
                ts[0] = scaled(0)
                add(0)
                ts[1] = scaled(1)
            for half in halves[k]:
                g = self.xg_lo(half)
            if k + 1 < KD:
                add(k + 1)
            if k + 2 < KD:
                ts[k + 2] = scaled(k + 2)
            return g

        return prepare

    def tables(self, name, off, reuse):
        t = self.FD[:, off:off + 1024]
        return t, self.sp.wait(*reuse).dma(t, self.ins[name][:, :], "tables")

    def scaled_tables(self, t, w, R, rw):
        self.dve.wait(w, rw).tt(t[:, 0:512], t[:, 0:512], R, ALU.mult)
        return self.dve.tt(t[:, 512:1024], t[:, 512:1024], R, ALU.mult, sig="tab_scaled")

    def rope_out(self, mark, bank, tab, tabw):
        A, B = self.tmp.next(), self.tmp.next()
        C, Sn = tab[:, 0:512], tab[:, 512:1024]
        self.dve.wait(mark, tabw, self.freed(A), self.freed(B)).tt(A.ap, bank.ap, C, ALU.mult)
        self.dve.tt(B.ap[64:128, :], bank.ap[0:64, :], Sn[0:64, :], ALU.mult)
        m = self.dve.tt(B.ap[0:64, :], bank.ap[64:128, :], Sn[64:128, :], ALU.mult, sig=bank.sem)
        return A, self.pool.wait(m).tt(A.ap, A.ap, B.ap, ALU.add, sig=B.sem)

    def split(self, hi, lo, src, after, reuse=None, eng=None, sig="split"):
        a = self.act.wait(after, reuse).act(hi, src, sig="split_hi")
        return (eng or self.pool).wait(a).tt(lo, src, hi.bitcast(F32), ALU.subtract, sig=sig)

    def silu2(self, g, bank, mark, R, rw, reuse=None):
        t = self.tmp.next()
        z = self.dve.wait(mark, rw, reuse).tt(g, bank.ap, R, ALU.mult, sig=bank.sem)
        a = self.act.wait(z, self.freed(t)).act(t.ap, g, scale=0.5, func=ACT.Tanh, sig="tanh")
        return self.dve.wait(a).stt(g, t.ap, 1.0, g, ALU.add, ALU.mult, sig=t.sem)

    def retention(self, xw):
        FR, FD, dve, act, pe, sp = self.FR, self.FD, self.dve, self.act, self.pe, self.sp
        D0 = 8192
        qk = [FR[:, D0 + 512 * i:D0 + 512 * i + 512] for i in range(4)]
        V = FR[:, D0 + 2048:D0 + 4096]
        Sb = FR[:, D0 + 4096:D0 + 4096 + 2560]
        Z = FR[:, D0 + 6656:D0 + 6656 + 16384]
        offs = [0, 512, 896, 1152]
        dec = [FD[:, 1024 + 512 * i:1536 + 512 * i] for i in range(2)]
        gates = [FD[:, 2048 + 512 * i:2560 + 512 * i] for i in range(4)]
        ON = FD[:, 4096:5120]
        gn = self.keep[:, 8:24]
        gnw = dve.wait(self.cold).ts(gn, self.cols[:, COLS["gn_gain_a"]:COLS["gn_gain_a"] + 16], 0.5, None, ALU.mult,
                                     sig="gn_half")
        pr, sr = Ring(self.bank[0:3]), Ring(self.bank[3:5])
        st, zw = {}, {}

        def prepare(k):
            g = self.xg_tile("g_pre_a", 0, k, xw[k])
            if k == 0:
                self.square(True, self.xt(0), None)
            if k + 1 < KD:
                self.square(False, self.xt(k + 1), xw[k + 1])
            return g

        def qk_out(n, mark, b):
            A, s = self.rope_out(mark, b, tab, st["tab"])
            return self.split(qk[2 * n], qk[2 * n + 1], A.ap, s, self.count("pe_scores"), sig=A.sem)

        def do_qk(h):
            st["qk"] = []
            for n in range(2):
                b = pr.next()
                mark = self.proj("w_in_a", h + 8 * n, KD, self.xin, b)
                st["qk"].append(qk_out(n, mark, b))

        def do_v(h):
            outs = self.proj_nat("w_in_a", [16 + 2 * h, 17 + 2 * h], KD, self.xin, pr)
            st["v"] = self.tokens_out(outs, st["y"], st["yw"], lambda t: (V[:, 256 * t:256 * t + 256],
                                                                         V[:, 1024 + 256 * t:1280 + 256 * t]),
                                      self.count("pe_values"))

        def gate_out(h, e, b, mark):
            g = gates[2 * (h % 2) + e]
            st[("g", h, e)] = (g, self.silu2(g, b, mark, self.R[:, :], st["rw"]))

        def do_gate(h):
            for e in range(2):
                b = pr.next()
                mark = self.proj("w_in_a", 32 + 2 * h + e, KD, self.xin, b)
                gate_out(h, e, b, mark)

        def load_decay(h):
            st[("dec", h)] = sp.wait(st.get(("masked", h - 2))).dma(dec[h % 2], self.ins["decay"][P * h:P * h + P, :],
                                                                   f"decay{h % 2}")

        def do_s(h):
            d, ld = dec[h % 2], st[("dec", h)]
            if h < 7:
                load_decay(h + 1)
            pe.wait(*st["qk"])
            values = self.count("pe_values")
            for j in range(4):
                b = sr.next()
                n = 512 - 128 * j
                kh, kl = qk[2][:, 128 * j:128 * j + 128], qk[3][:, 128 * j:128 * j + 128]
                qh, ql = qk[0][:, 128 * j:512], qk[1][:, 128 * j:512]
                pe.wait(self.freed(b))
                mark = self.group(b.ap[:, 0:n], [(kh, qh), (kh, ql), (kl, qh)], sig="pe_scores")
                t = self.tmp.next()
                m = dve.wait(mark, ld, self.freed(t)).tt(t.ap[:, 0:n], b.ap[:, 0:n], d[:, 0:n], ALU.mult,
                                                         sig=b.sem)
                o = offs[j]
                st["s"] = self.split(Sb[:, o:o + n], Sb[:, 1280 + o:1280 + o + n], t.ap[:, 0:n], m, values, sig=t.sem)
                st[("s", j)] = st["s"]
            st[("masked", h)] = m

        def do_o(h):
            mv, var, rs = self.small(8), self.small(4), self.small(4)
            marks = []
            pe.wait(st["v"])
            for i in range(4):
                b = self.bank[5 + i // 2]
                if i % 2 == 0:
                    pe.wait(self.freed(b))
                terms = []
                for j in range(i + 1):
                    o = offs[j] + 128 * (i - j)
                    sh, sl = Sb[:, o:o + 128], Sb[:, 1280 + o:1280 + o + 128]
                    vh, vl = V[:, 256 * j:256 * j + 256], V[:, 1024 + 256 * j:1280 + 256 * j]
                    terms += [(sh, vh), (sl, vh), (sh, vl)]
                pe.wait(st[("s", i)])
                marks.append(self.group(b.ap[:, 256 * (i % 2):256 * (i % 2) + 256], terms, sig="pe_values"))
            for i in range(4):
                ap = self.bank[5 + i // 2].ap[:, 256 * (i % 2):256 * (i % 2) + 256]
                s6, m2 = self.small(6), mv[:, 2 * i:2 * i + 2]
                d = dve.wait(marks[i | 1]).do(lambda e, s6=s6, ap=ap: e.bn_stats(s6, ap), "bn")
                d = dve.wait(d).do(lambda e, s6=s6, m2=m2: e.bn_aggr(m2, s6), "bn")
            vs = mv.rearrange("p (i t) -> p i t", t=2)[:, :, 1]
            d = dve.wait(d).ts(var, vs, EPS, None, ALU.add, sig="bn")
            d = self.newton(var, rs, d)
            dve.wait(d, self.count("pe_turn_o"))
            for i in range(4):
                b = self.bank[5 + i // 2]
                d = dve.ts(ON[:, 256 * i:256 * i + 256], b.ap[:, 256 * (i % 2):256 * (i % 2) + 256],
                           mv[:, 2 * i:2 * i + 1], rs[:, i:i + 1], ALU.subtract, ALU.mult,
                           sig=b.sem if i % 2 else None)
            st["on"] = d

        def do_t(h):
            pe.wait(st["on"])
            for e in range(2):
                b = self.bank[7] if e == 0 else pr.next() if h < 7 else self.bank[4]
                pe.wait(self.freed(b))
                for i in range(4):
                    mark = pe.turn(b.ap[:, 128 * i:128 * i + 128], ON[:, 256 * i + 128 * e:256 * i + 128 * e + 128],
                                   self.ident[:, :], sig="pe_turn_o")
                g, z = st[("g", h, e)]
                t = self.tmp.next()
                k = 2 * h + e
                m = dve.wait(mark, z, gnw, self.freed(t)).stt(t.ap, b.ap, gn[:, k:k + 1], g, ALU.mult, ALU.mult,
                                                              sig=b.sem)
                zw[k] = self.split(Z[:, 512 * k:512 * k + 512], Z[:, 8192 + 512 * k:8704 + 512 * k], t.ap, m,
                                   sig=t.sem)

        tab, tw = self.tables("rope_a", 0, [])
        wide = self.bank[0:4]
        marks, st["y"], st["yw"], R, st["rw"] = self.entry([("w_in_a", c, self.xin) for c in (0, 8, 32, 33)], wide,
                                                           prepare)
        st["tab"] = self.scaled_tables(tab, tw, R, st["rw"])
        st["qk"] = [qk_out(n, marks[n], wide[n]) for n in range(2)]
        for e in range(2):
            gate_out(0, e, wide[2 + e], marks[2 + e])
        load_decay(0)
        do_v(0)
        for h in range(8):
            do_s(h)
            if h:
                do_t(h - 1)
            if h < 7:
                do_qk(h + 1)
            do_o(h)
            if h < 7:
                do_v(h + 1)
                do_gate(h + 1)
        self.out_proj("w_out_a", 16, lambda p, k: Z[:, 8192 * p + 512 * k:8192 * p + 512 * k + 512], zw,
                      lambda: [self.count("pe_turn_o"), zw[15]], None, {2: lambda: do_t(7)})

    def latent(self, residual):
        FR, FD, dve, act, pe, sp = self.FR, self.FD, self.dve, self.act, self.pe, self.sp
        D0 = 8192

        def fr(o, n):
            return FR[:, D0 + o:D0 + o + n]

        ckv, cq, kr = fr(0, 2048), fr(2048, 3072), fr(5120, 2048)
        kb = Ring([fr(7168 + 1024 * i, 1024) for i in range(2)])
        vb = Ring([fr(9216 + 2048 * i, 2048) for i in range(2)])
        qn = Ring([fr(13312 + 1024 * i, 1024) for i in range(2)])
        qr = Ring([fr(15360 + 1024 * i, 1024) for i in range(2)])
        pt = Slot(fr(17408, 4096), "pt")
        Z = FR[:, 0:8192]
        gate = [FD[:, 512 * i:512 * i + 512] for i in range(8)]
        scale = 192 ** -0.5
        tab, tw = self.tables("rope_b", 4096, [self.y_last])
        pr = Ring(self.bank[0:6])
        t = self.tmp.next()
        mk = sp.wait(self.freed(t)).dma(t.ap[:, 0:128], self.ins["mask"][:, :], "mask")
        act.wait(self.y_last, mk).act(self.MK[:, 0:128], self.ident[:, :])
        mkw = act.act(self.MK[:, 128:256], t.ap[:, 0:128], sig=t.sem)

        def scaled(c, name, m, hi, lo, after, sig):
            g = self.col(name, m)
            a = act.wait(after).act(hi, c, scale=g, sig="lat_hi")
            return dve.wait(a).stt(lo, c, g, hi.bitcast(F32), ALU.mult, ALU.subtract, sig=sig)

        def xin_b(p, k):
            return fr(7168 + 4096 * p + 512 * k, 512)

        wide = [pr.next() for _ in range(6)]
        ropec = [256 + i % 32 + 32 * (i // 64) for i in range(128)]
        marks, y, yw, R, rw = self.entry([("w_kv_a", c, self.xin) for c in (0, 1, ropec)] +
                                         [("w_in_b", c, xin_b) for c in range(3)], wide,
                                         self.into(residual, [("g_kv", 0, 0), ("g_pre_b", 0, D0 + 7168)],
                                                   self.y_last), at=6)
        cs, sq = [], None
        for m in range(2):
            c = self.tmp.next()
            z = dve.wait(marks[m], rw, self.freed(c)).tt(c.ap, wide[m].ap, R, ALU.mult, sig=wide[m].sem)
            sq = self.square(m == 0, c.ap, z)
            cs.append(scaled(c.ap, "g_kv_lat", m, ckv[:, 512 * m:512 * m + 512],
                             ckv[:, 1024 + 512 * m:1536 + 512 * m], z, c.sem))
        tabw = self.scaled_tables(tab, tw, R, rw)
        A, s = self.rope_out(marks[2], wide[2], tab, tabw)
        for par in range(2):
            o = 1024 * par
            hi, lo = kr[:, o:o + 512], kr[:, o + 512:o + 1024]
            mk = self.masks[:, par:par + 1]
            a = act.wait(s).act(hi, A.ap, scale=mk, sig="lat_hi")
            krw = dve.wait(a).stt(lo, A.ap, mk, hi.bitcast(F32), ALU.mult, ALU.subtract, sig=A.sem if par else None)
        cqw, cs3, kv_squares = [], [], sq
        for m in range(3):
            c, b = self.tmp.next(), wide[3 + m]
            cs3.append((c, dve.wait(marks[3 + m], self.freed(c)).tt(c.ap, b.ap, R, ALU.mult, sig=b.sem)))
        for m in range(3):
            c, z = cs3[m]
            cqw.append(scaled(c.ap, "g_q_lat", m, cq[:, 512 * m:512 * m + 512],
                              cq[:, 1536 + 512 * m:2048 + 512 * m], z, "q_lat"))
        gw = []
        tw2 = sp.wait(krw).dma(tab, self.ins["rope_b"][:, :], "tables")
        for m in range(8):
            b = pr.next()
            mark = self.proj("w_in_b", 3 + m, KD, xin_b, b)
            if m == 0:
                sums = self.token_sums(kv_squares)
                act.wait(sums)
                for i in range(3):
                    sq = self.square(i == 0, cs3[i][0].ap, cqw[i], cs3[i][0].sem)
            elif m == 2:
                x = self.spread(y2, y2w)
                R2, r2w = self.R2[:, :], act.wait(x).act(self.R2[:, :], self.bank[6].ap, sig=self.bank[6].sem)
            elif m == 4:
                sums = self.token_sums(sq)
            gw.append(self.silu2(gate[m], b, mark, R, rw, self.y_read if m == 0 else None))
            if m == 0:
                y2, y2w = self.rms(sums, 256)
            elif m == 4:
                y3, y3w = self.rms(sums, 384)
        xg_read = mark
        m = self.spread(y3, y3w)
        r3w = act.wait(m, gw[-1]).act(self.R[:, :], self.bank[6].ap, sig=self.bank[6].sem)
        R3 = self.R[:, :]
        tabw3 = self.scaled_tables(tab, tw2, R3, r3w)
        pr, srg = Ring(self.bank[0:2]), Ring(self.bank[2:5])
        ptr, ob = Ring(self.bank[5:7]), Ring(self.bank[7:8])

        def kin(p, k):
            return ckv[:, 1024 * p + 512 * k:1024 * p + 512 * k + 512]

        def qin(p, k):
            return cq[:, 1536 * p + 512 * k:1536 * p + 512 * k + 512]

        st, zw = {}, {}
        every, probs = self.tmp, Ring(self.tmp.slots[0:4])
        squares = Slot(self.acc[:, :], "td")
        self.tmp = Ring(every.slots[4:6] + [squares])
        dve.wait(y3w)
        act.wait(xg_read)

        def rope_pair(h):
            b = pr.next()
            c0 = [192 * (h + i // 32 % 2) + 128 + 32 * (i // 64) + i % 32 for i in range(128)]
            mark = self.proj("w_uq", c0, 3, qin, b, cqw)
            A, s = self.rope_out(mark, b, tab, tabw3)
            q = qr.next()
            st["qr"] = (q, self.split(q[:, 0:512], q[:, 512:1024], A.ap, s, st.get(("S", h - 3)), sig=A.sem))

        def value_pair(h):
            v = vb.next()
            if len(self.order) % 2:
                self.order.append(None)
            outs = self.proj_nat("w_uv", [h, h + 1], 2, kin, pr, cs)
            st["v"] = (v, self.tokens_out(outs, y2, y2w, lambda t: (v[:, 256 * t:256 * t + 256],
                                                                    v[:, 1024 + 256 * t:1280 + 256 * t]),
                                          self.count("pt")))

        def head_tile(h, name, cols, K, xi, ready, ring, Rr, rr):
            b = pr.next()
            mark = self.proj(name, cols, K, xi, b, ready)
            t = self.tmp.next()
            d = dve.wait(mark, rr, self.freed(t)).tt(t.ap, b.ap, Rr, ALU.mult, sig=b.sem)
            o = ring.next()
            return o, self.split(o[:, 0:512], o[:, 512:1024], t.ap, d, st.get(("S", h - 2)), sig=t.sem)

        def key_tile(h):
            st["k"] = head_tile(h, "w_uk", h, 2, kin, cs, kb, R2, r2w)

        def query_tile(h):
            st["q"] = head_tile(h, "w_uq", list(range(192 * h, 192 * h + 128)), 3, qin, cqw, qn, R3, r3w)

        def settle(h):
            st[h] = dict(st)

        def scores(h, i):
            (q, qw), (k, kw), (qq, qqw) = st[h]["q"], st[h]["k"], st[h]["qr"]
            o = 1024 * (h % 2)
            mx, nm, rs = self.small(1), self.small(1), self.small(1)
            pe.wait(*((qw, kw, qqw, krw, mkw) if i == 0 else ()))
            n = 128 * (i + 1)
            b = srg.next()
            sl = slice(128 * i, 128 * i + 128)
            qh, ql = q[:, sl], q[:, 512 + 128 * i:640 + 128 * i]
            rh, rl = qq[:, sl], qq[:, 512 + 128 * i:640 + 128 * i]
            kh, kl = k[:, 0:n], k[:, 512:512 + n]
            th, tl = kr[:, o:o + n], kr[:, o + 512:o + 512 + n]
            pe.wait(self.freed(b))
            terms = [(rh, th), (rh, tl), (rl, th), (qh, kh), (qh, kl)]
            self.group(b.ap[:, 0:n], terms, True, False)
            self.group(b.ap[:, n - 128:n], [(self.MK[:, 0:128], self.MK[:, 128:256])], False, False)
            mark = self.group(b.ap[:, 0:n], [(ql, kh)], False, True, "pe_scores")
            d = dve.wait(mark).do(lambda e: e.tensor_reduce(mx, b.ap[:, 0:n], AXX, ALU.max), "row_max")
            d = dve.wait(d).ts(nm, mx, -scale, None, ALU.mult, sig="row_max")
            t = probs.next()
            a = act.wait(d, self.freed(t)).act(t.ap[:, 0:n], b.ap[:, 0:n], scale=scale, func=ACT.Exp, bias=nm,
                                               accum=rs, sig=b.sem)
            st[("E", h, i)] = (t, rs, a)
            st[("S", h)] = mark

        def divide(h, i):
            t, rs, a = st[("E", h, i)]
            n = 128 * (i + 1)
            d = dve.wait(a).do(lambda e: e.reciprocal(rs, rs), "row_rec")
            d = dve.wait(d).ts(t.ap[:, 0:n], t.ap[:, 0:n], rs, None, ALU.mult, sig="probs")
            st[("P", h, i)] = (t, d)

        def turn(h, i):
            if i == 0:
                st["pt_free"] = self.freed(pt)
            t, d = st[("P", h, i)]
            sl = slice(128 * i, 128 * i + 128)
            hi, lo = [pt.ap[:, 2048 * p:2048 * p + 2048].rearrange("p (j c) -> p j c", c=512)[:, 0:i + 1, sl]
                      for p in range(2)]
            st["T"] = self.turn_tile(t, d, i, ptr.next(), hi, lo, st["pt_free"])

        def values(h):
            v, vw = st[h]["v"]
            b = ob.next()
            c = 128 * (h % 2)
            pe.wait(st["T"], vw, self.freed(b))
            for j in range(4):
                vh = v[:, 256 * j + c:256 * j + c + 128]
                vl = v[:, 1024 + 256 * j + c:1152 + 256 * j + c]
                ph, pl = pt.ap[:, 640 * j:512 * j + 512], pt.ap[:, 2048 + 640 * j:2560 + 512 * j]
                mark = self.group(b.ap[:, 128 * j:512], [(vh, ph), (vl, ph), (vh, pl)], j == 0, j == 3,
                                  "pt" if j == 3 else None)
            t = self.tmp.next()
            d = dve.wait(mark, gw[h], self.freed(t)).stt(t.ap, b.ap, 0.5, gate[h], ALU.mult, ALU.mult, sig=b.sem)
            zw[h] = self.split(Z[:, 512 * h:512 * h + 512], Z[:, 4096 + 512 * h:4608 + 512 * h], t.ap, d, xg_read,
                               sig=t.sem)
            self.gate_read = d

        rope_pair(0)
        key_tile(0)
        query_tile(0)
        settle(0)
        value_pair(0)
        st[0]["v"] = st["v"]
        def last_turn():
            divide(7, 3)
            turn(7, 3)

        def last_values():
            values(7)
            self.tmp = every

        for h in range(8):
            after, even = h < 7, h % 2 == 1
            scores(h, 0)
            if h:
                divide(h - 1, 3)
                turn(h - 1, 3)
            if after and even:
                rope_pair(h + 1)
            if after and not even:
                key_tile(h + 1)
            scores(h, 1)
            divide(h, 0)
            if h:
                values(h - 1)
            if after and even:
                key_tile(h + 1)
            if after:
                query_tile(h + 1)
            scores(h, 2)
            divide(h, 1)
            turn(h, 0)
            if after and even:
                value_pair(h + 1)
            if after:
                settle(h + 1)
            scores(h, 3)
            divide(h, 2)
            turn(h, 1)
            turn(h, 2)
        self.out_proj("w_out_b", 8, lambda p, k: Z[:, 4096 * p + 512 * k:4096 * p + 512 * k + 512], zw,
                      lambda: [self.gate_read, self.freed(squares)], None, {0: last_turn, 2: last_values})

    def turn_tile(self, t, d, i, b, hi, lo, reuse):
        n = 128 * (i + 1)
        self.pe.wait(d, self.freed(b))
        for j in range(i + 1):
            mark = self.pe.turn(b.ap[:, 128 * j:128 * j + 128], t.ap[:, 128 * j:128 * j + 128], self.ident[:, :],
                                sig=t.sem if j == i else None)
        src = b.ap[:, 0:n]
        if len(hi.shape) == 3:
            src = src.rearrange("p (j c) -> p j c", c=128)
        a = self.act.wait(mark, reuse).act(hi, src, sig="pt_hi")
        return self.dve.wait(a).tt(lo, src, hi.bitcast(F32), ALU.subtract, sig=b.sem)

    def tap(self, u, uw, out, w):
        return self.act.wait(uw, self.freed(out)).act(out.ap, u, scale=w, sig="tap")

    def taps(self, u, after, out, w, sig):
        b = self.dve.wait(after).stt(out.ap[:, 1:512], u[:, 0:511], w[1], out.ap[:, 1:512], ALU.mult, ALU.add,
                                     sig="tap1")
        return self.dve.wait(b).stt(out.ap[:, 2:512], u[:, 0:510], w[0], out.ap[:, 2:512], ALU.mult, ALU.add,
                                    sig=sig)

    def mixer(self, residual):
        FR, dve = self.FR, self.dve
        E = FR[:, 8192:16384]
        pr = Ring(self.bank[0:6])
        ew = {}
        oh, rb = self.FD[0:33, 4096:4736], self.FD[0:33, 4736:4744]
        self.sp.wait(self.gate_read).dma(rb, self.ins["rb"][:, :], "bias_in")
        self.scrw = []
        self.bias_in = oh, rb, self.sp.dma(oh, self.ins["onehot"][:, :], "bias_in")
        y6 = [pr.next() for _ in range(6)]
        marks6, y, yw, R, rw = self.entry([("w_sc_in_2", c, self.xin) for c in (8, 16, 0, 9, 17, 1)], y6,
                                          self.into(residual, [("g_pre_mix_2", 0, 0)], self.y_last))
        R2 = self.R2[:, :]
        r2 = dve.wait(rw).tt(R2, R, R, ALU.mult, sig="r_squared")
        slots, self.tmp = self.tmp, Ring(self.tmp.slots + self.y_slots)
        dve.wait(self.y_read)
        half = {}

        def front(m, banks, marks):
            a, g, o = self.tmp.next(), self.tmp.next(), self.tmp.next()
            x = dve.wait(marks[0], r2, self.freed(a)).tt(a.ap, banks[0].ap, R2, ALU.mult, sig=banks[0].sem)
            z = dve.wait(marks[2], self.freed(g)).tt(g.ap, banks[2].ap, R, ALU.mult, sig=banks[2].sem)
            x = dve.wait(marks[1], x).tt(a.ap, banks[1].ap, a.ap, ALU.mult, sig=banks[1].sem)
            half[m] = (a, g, z, o, self.tap(a.ap, x, o, self.col("w_sc_conv_2", 16 + m)))

        def back(m):
            a, g, z, o, v = half[m]
            v = self.taps(a.ap, v, o, [self.col("w_sc_conv_2", 8 * t + m) for t in range(2)], a.sem)
            x = dve.wait(z, v).tt(g.ap, g.ap, o.ap, ALU.mult, sig=o.sem)
            ew[m] = self.split(E[:, 512 * m:512 * m + 512], E[:, 4096 + 512 * m:4608 + 512 * m], g.ap, x, sig=g.sem)

        for m in range(8):
            if m < 2:
                front(m, y6[3 * m:3 * m + 3], marks6[3 * m:3 * m + 3])
            else:
                banks = [pr.next() for _ in range(3)]
                front(m, banks, [self.proj("w_sc_in_2", c, KD, self.xin, b) for c, b in zip((8 + m, 16 + m, m), banks)])
            if m:
                back(m - 1)
            self.bias_table(m)
        back(7)
        self.tmp = slots
        self.out_proj("w_sc_out_2", 8, lambda p, k: E[:, 4096 * p + 512 * k:4096 * p + 512 * k + 512], ew,
                      lambda: [self.freed(t) for t in self.y_slots], pr)

    def ffn(self, L, residual):
        FR, dve, act = self.FR, self.dve, self.act
        M = FR[:, 8192:8192 + 2 * NF * 512]
        pr = Ring(self.bank[0:6])
        name = f"w_ffn_up_2_{L}"
        mw = {}

        def taps(ch):
            return [self.col("w_ffn_conv_2", L * 132 + t * 44 + ch) for t in range(3)]

        half = {}

        def front(m, banks, marks):
            us = []
            for i in range(2):
                u = self.tmp.next()
                us.append((u, dve.wait(marks[i], rw, self.freed(u)).tt(u.ap, banks[i].ap, R, ALU.mult,
                                                                       sig=banks[i].sem)))
            half[m] = []
            for i, (u, x) in enumerate(us):
                o = self.tmp.next()
                half[m].append((u, o, self.tap(u.ap, x, o, taps(m + NF * i)[2])))

        def back(m):
            (u0, c0, v0), (u1, c1, v1) = half[m]
            v0 = self.taps(u0.ap, v0, c0, taps(m), u0.sem)
            t = self.tmp.next()
            a = act.wait(v0, self.freed(t)).act(t.ap, c0.ap, scale=0.5, func=ACT.Tanh, sig="tanh")
            v1 = self.taps(u1.ap, v1, c1, taps(m + NF), u1.sem)
            x = dve.wait(a).stt(t.ap, t.ap, 1.0, c0.ap, ALU.add, ALU.mult, sig=c0.sem)
            x = dve.wait(x, v1).stt(t.ap, t.ap, 0.5, c1.ap, ALU.mult, ALU.mult, sig=c1.sem)
            mw[m] = self.split(M[:, 512 * m:512 * m + 512], M[:, (NF + m) * 512:(NF + m) * 512 + 512], t.ap, x,
                               self.y_last if m == 0 else None, sig=t.sem)

        y6 = [pr.next() for _ in range(6)]
        marks6, y, yw, R, rw = self.entry([(name, c, self.xin) for c in (0, NF, 1, NF + 1, 2, NF + 2)], y6,
                                          self.into(residual, [("g_pre_ffn_2", 8 * L, 0)], self.y_last))
        slots, self.tmp = self.tmp, Ring(self.tmp.slots + self.y_slots)
        dve.wait(self.y_read)
        for m in range(NF):
            if m < 3:
                front(m, y6[2 * m:2 * m + 2], marks6[2 * m:2 * m + 2])
            else:
                if m == NF - 1:
                    loads = self.p_load(L)
                banks = [pr.next(), pr.next()]
                marks = [self.proj(name, m, KD, self.xin, banks[0]), self.proj(name, NF + m, KD, self.xin, banks[1])]
                front(m, banks, marks)
            if m:
                back(m - 1)
        back(NF - 1)
        self.tmp = slots
        self.pw = self.p_operand(loads, self.FR[:, 3072:4096], self.FR[:, 7168:8192], marks[1])
        self.out_proj(f"w_ffn_down_2_{L}", NF, lambda p, k: M[:, (NF * p + k) * 512:(NF * p + k) * 512 + 512], mw,
                      lambda: [self.freed(t) for t in self.y_slots], pr)

    def p_load(self, L):
        loads = []
        for k in range(2):
            t = self.tmp.next()
            loads.append((t, self.sp.wait(self.freed(t)).dma(
                t.ap, self.ins["pT"][256 * L + 128 * k:256 * L + 128 * k + 128, :], f"p{k}")))
        return loads

    def p_operand(self, loads, hi, lo, reuse):
        marks = []
        for k in range(2):
            t, ld = loads[k]
            marks.append(self.split(hi[:, 512 * k:512 * k + 512], lo[:, 512 * k:512 * k + 512], t.ap, ld, reuse,
                                    eng=self.dve, sig=t.sem))
        return marks

    def ple(self, L):
        FR, dve, act = self.FR, self.dve, self.act
        pw, at = self.pw, (3072, 7168)

        def pin(p, k):
            return FR[:, at[p] + 512 * k:at[p] + 512 * k + 512]

        pr = Ring(self.bank[0:6])
        proj = {}

        def project(m):
            proj[m] = (b := pr.next(), self.proj(f"w_ple_proj_2_{L}", m, 2, pin, b, pw if m in (0, 3) else None))
            if m < 3:
                k = (self.FD[:, 4096:4608], self.FD[:, 4608:5120], self.R2[:, :])[m]
                if m == 0:
                    for a in range(2):
                        act.wait(self.y_last, *pw).act(FR[:, 8192 + 1024 * a:9216 + 1024 * a],
                                                       FR[:, at[a]:at[a] + 1024].bitcast(F32), sig="p_copy")
                proj[m] = (Slot(k, "ple_kept"), act.wait(proj[m][1], self.count("ple_kept")).act(k, b.ap, sig=b.sem))

        residual = self.normed(1024, "g_post_ffn_2", 8 * L, 1.0, [lambda m=m: project(m) for m in range(3)])
        filled = self.count("pe_proj")
        wide = [pr.next() for _ in range(6)]
        marks, y, yw, R, rw = self.entry([(f"w_ple_gate_2_{L}", c, self.xin) for c in range(6)], wide,
                                         self.into(residual, [("g_pre_ple_2", 8 * L, 0)], filled))
        pw, at = [self.count("p_copy")] * 2, (8192, 9216)
        dve.wait(self.y_read)
        for m in range(8):
            if m < 6:
                b0, r0 = wide[m], marks[m]
            else:
                b0 = pr.next()
                r0 = self.proj(f"w_ple_gate_2_{L}", m, KD, self.xin, b0)
            if m > 2:
                project(m)
            b1, r1 = proj[m]
            t = self.tmp.next()
            x = dve.wait(r0, rw, self.freed(t)).tt(t.ap, b0.ap, R, ALU.mult, sig=b0.sem)
            a = act.wait(x).act(t.ap, t.ap, scale=0.5, func=ACT.Tanh, sig="tanh")
            x = dve.wait(a, r1).stt(self.Y[m], t.ap, 1.0, b1.ap, ALU.add, ALU.mult, sig=b1.sem)
            if m < 7:
                self.acc_mark = self.square(m == 0, self.Y[m], x, t.sem)
            else:
                t7 = self.tmp.next()
                self.last_square = (t7, act.wait(x, self.freed(t7)).act(t7.ap, self.Y[m], func=ACT.Square, sig=t.sem))
            self.y_mark = x
        self.y_last = r0
        return self.normed(4096, "g_post_ple_2", 8 * L, 0.5)

    def bias_table(self, h):
        sp, pe, act = self.sp, self.pe, self.act
        scr = self.ins["scr"]
        oh, rb, ld = self.bias_in
        pe.wait(ld)
        for i in range(2):
            b, t = self.bank[6 + i], self.tmp.next()
            pe.wait(self.freed(b))
            m = pe.mm(b.ap[:, 0:320], rb[:, h:h + 1].broadcast_to([33, P]), oh[:, 320 * i:320 * i + 320], True, True,
                      sig="pe_bias")
            a = act.wait(m, self.freed(t)).act(t.ap[:, 0:320], b.ap[:, 0:320], scale=8.0, sig=b.sem)
            dst = bass.AP(scr.tensor, h * P * (TW + 1) + 320 * i, [[TW + 1, P], [1, 320]])
            self.scrw.append(sp.wait(a).dma(dst, t.ap[:, 0:320], t.sem))

    def diff(self, residual):
        FR, FD, dve, act, pe, sp = self.FR, self.FD, self.dve, self.act, self.pe, self.sp
        D0 = 8192
        KZ, V = FR[:, D0:D0 + 8192], FR[:, D0 + 8192:D0 + 16384]
        qb = Ring([Slot(FR[:, D0 + 16384 + 2048 * i:D0 + 18432 + 2048 * i], f"qb{i}") for i in range(2)])
        pt = Slot(FR[:, D0 + 20480:D0 + 23040], "pt")
        TB = FD[:, 0:4096].rearrange("p (h c) -> p h c", h=8)
        extra = [Slot(FD[:, 4096:4608], "ta"), Slot(FD[:, 4608:5120], "tb"), Slot(self.R2[:, :], "tc"),
                 Slot(self.acc[:, :], "td")]
        pr = Ring(self.bank[0:6])
        kw, vw = {}, {}
        wide = [pr.next() for _ in range(6)]
        marks, y, yw, R, rw = self.entry([("w_kv_2", c, self.xin) for c in range(6)], wide,
                                         self.into(residual, [("g_kv_2", 0, 0)], self.y_last))
        lv = self.tmp.next()
        ld = sp.wait(self.freed(lv)).dma(lv.ap[:, 0:256], bass.AP(self.ins["lam"].tensor, 0, [[0, P], [1, 256]]),
                                         "lam")
        d2, e2, lam, gs = self.keep[:, 0:2], self.keep[:, 2:4], self.keep[:, 4:5], self.keep[:, 5:6]
        dve.wait(ld)
        for i in range(2):
            o = 128 * i
            x = dve.tt(lv.ap[:, 256 + 64 * i:320 + 64 * i], lv.ap[:, o:o + 64], lv.ap[:, o + 64:o + 128], ALU.mult,
                       sig="lam_dve")
        x = dve.wait(x).do(lambda e: e.tensor_reduce(d2, lv.ap[:, 256:384].rearrange("p (a b) -> p a b", a=2), AXX,
                                                     ALU.add), lv.sem)
        a = act.wait(x).act(e2, d2, func=ACT.Exp, sig="lam_act")
        x = dve.wait(a).tt(lam, e2[:, 1:2], e2[:, 0:1], ALU.subtract, sig="lam_dve")
        lamw = dve.wait(x).ts(lam, lam, -LAMBDA_INIT, None, ALU.add, sig="lam_dve")
        gsw = dve.ts(gs, self.col("g_subln_2", 0), 1.0 - LAMBDA_INIT, None, ALU.mult, sig="lam_dve")
        for h in range(8):
            if h < 6:
                b, mark = wide[h], marks[h]
            else:
                b = pr.next()
                mark = self.proj("w_kv_2", h, KD, self.xin, b)
            t = self.tmp.next()
            d = dve.wait(mark, rw, self.freed(t)).tt(t.ap, b.ap, R, ALU.mult, sig=b.sem)
            kw[h] = self.split(KZ[:, 1024 * h:1024 * h + 512], KZ[:, 1024 * h + 512:1024 * h + 1024], t.ap, d,
                               sig=t.sem)
        for b in qb.slots:
            for p in range(2):
                o = 1024 * p
                half = slice(64, 128) if p == 0 else slice(0, 64)
                zq = dve.do(lambda e, b=b, o=o, half=half: e.memset(b.ap[half, o:o + 1024].bitcast(F32), 0.0),
                            "zero_q")
        src = bass.AP(self.ins["scr"].tensor, P - 1, [[TW, P], [P * (TW + 1), 8], [1, 512]])
        tbw = sp.wait(*self.scrw, self.y_read).dma(TB, src, "bias_table")
        for c in range(4):
            outs = self.proj_nat("w_kv_2", [8 + 2 * c, 9 + 2 * c], KD, self.xin, pr)
            vw[c] = self.tokens_out(outs, y, yw, lambda t: (V[:, 1024 * t + 256 * c:1024 * t + 256 * c + 256],
                                                           V[:, 4096 + 1024 * t + 256 * c:4352 + 1024 * t + 256 * c]),
                                    None)
        xg_read = self.unit_end[(len(self.order) - 1) // UNIT]
        xq = [self.xg_tile("g_pre_mix_2", 8, k, None, xg_read if k == 0 else None) for k in range(KD)]
        pr, srg = Ring(self.bank[0:1]), Ring(self.bank[1:5])
        ptr, ob, last = Ring(self.bank[5:6]), Ring(self.bank[6:7]), self.bank[7]
        dve.wait(self.count("ple_kept"), yw)
        act.wait(self.count("ple_kept"), yw)
        slots, self.tmp = self.tmp, Ring(self.tmp.slots + extra)
        offs = [0, 512, 896, 1152]
        st, zw = {"pool": kw[7]}, {}

        def project(h):
            b = pr.next()
            mark = self.proj("w_q_2", h, KD, self.xin, b, xq if h == 0 else None)
            t = self.tmp.next()
            d = dve.wait(mark, self.freed(t)).tt(t.ap, b.ap, R, ALU.mult, sig=b.sem)
            q = qb.next()
            act.wait(d, self.freed(q))
            for p in range(2):
                hs, o = slice(64 * p, 64 * p + 64), 1024 * p
                a = act.act(q.ap[hs, o:o + 512], t.ap[hs, :], sig="q_hi")
            w = st["pool"]
            self.pool.wait(a)
            for p in range(2):
                hs, o = slice(64 * p, 64 * p + 64), 1024 * p
                w = self.pool.wait(w).tt(q.ap[hs, o + 512:o + 1024], t.ap[hs, :], q.ap[hs, o:o + 512].bitcast(F32),
                                         ALU.subtract, sig=t.sem if p else "q_lo")
            st["pool"], st[h] = w, (q, w)

        def scores(h, i):
            q, qw = st[h]
            n = 128 * (i + 1)
            if i == 0:
                st[("s", h)] = (self.small(4), self.small(4))
            mx, w, sums = self.small(2), self.small(1), st[("s", h)]
            Ps = []
            kh, kl = KZ[:, 1024 * h:1024 * h + n], KZ[:, 1024 * h + 512:1024 * h + 512 + n]
            if i == 0:
                pe.wait(qw, kw[h], zq)
                dve.wait(tbw)
            for p in range(2):
                b = srg.next()
                o = 1024 * p + 128 * i
                qh, ql = q.ap[:, o:o + 128], q.ap[:, o + 512:o + 640]
                pe.wait(self.freed(b))
                mark = self.group(b.ap[:, 0:n], [(qh, kh), (qh, kl), (ql, kh)],
                                  sig=q.sem if (i, p) == (3, 1) else "pe_scores")
                t = self.tmp.next()
                m = mx[:, p:p + 1]
                d = dve.wait(mark, self.freed(t)).do(
                    lambda e, t=t, b=b, m=m: e.tensor_tensor_reduce(t.ap[:, 0:n], b.ap[:, 0:n], TB[:, h, 512 - n:512],
                                                                    -0.125, 3.0e38, ALU.add, ALU.min, m), b.sem)
                Ps.append((t, d))
            act.wait(d)
            for p in range(2):
                t = Ps[p][0]
                a = act.act(t.ap[:, 0:n], t.ap[:, 0:n], scale=-1.0, func=ACT.Exp, bias=mx[:, p:p + 1],
                            accum=sums[p][:, i:i + 1], sig="exp")
            st[("E", h, i)] = (Ps[0][0], Ps[1][0], a, w)
            st[("sl", h)] = mark

        def combine(h, i):
            t0, t1, a, w = st[("E", h, i)]
            sums, n = st[("s", h)], 128 * (i + 1)
            s0, s1 = sums[0][:, i:i + 1], sums[1][:, i:i + 1]
            d = dve.wait(a).do(lambda e: e.reciprocal(w, s1), "row_rec")
            d = dve.wait(d, lamw).stt(w, s0, lam, w, ALU.mult, ALU.mult, sig="row_rec")
            x = dve.wait(d).stt(t0.ap[:, 0:n], t1.ap[:, 0:n], w, t0.ap[:, 0:n], ALU.mult, ALU.add, sig=t1.sem)
            st[("P", h, i)] = (t0, x)

        def turn(h, i):
            t, d = st.pop(("P", h, i))
            if i == 0:
                st["pt_free"] = self.freed(pt)
            b = ptr.next()
            pe.wait(d, self.freed(b))
            for j in range(i + 1):
                mark = pe.turn(b.ap[:, 128 * j:128 * j + 128], t.ap[:, 128 * j:128 * j + 128], self.ident[:, :],
                               sig=t.sem if j == i else None)
            ends = [(j, min(j + 2, i + 1)) for j in range(0, i + 1, 2)]
            act.wait(mark, st["pt_free"])
            for part in range(2):
                for j, e in ends:
                    o = offs[j] + 128 * (i - j) + 1280 * part
                    step = offs[j + 1] - offs[j] - 128 if e - j == 2 else 128
                    out = pt.ap[:, o:o + 128] if e - j == 1 else bass.AP(
                        pt.ap.tensor, pt.ap.offset + o, [list(pt.ap.ap[0]), [step, 2], [1, 128]])
                    src = b.ap[:, 128 * j:128 * e]
                    if e - j == 2:
                        src = src.rearrange("p (j c) -> p j c", c=128)
                    if part == 0:
                        a = act.act(out, src, sig="pt_hi")
                        st[("hi", j)] = out
                    else:
                        x = dve.wait(a).tt(out, src, st[("hi", j)].bitcast(F32), ALU.subtract,
                                           sig=b.sem if e == i + 1 else "pt_lo")
            st[("T", h)] = x

        def values(h):
            b = ob.next()
            pe.wait(st[("T", h)], vw[h // 2], self.freed(b))
            for j in range(4):
                o, c = offs[j], 1024 * j + 128 * h
                ph, pl = pt.ap[:, o:o + 512 - 128 * j], pt.ap[:, 1280 + o:1792 + o - 128 * j]
                vh, vl = V[:, c:c + 128], V[:, 4096 + c:4224 + c]
                mark = self.group(b.ap[:, 128 * j:512], [(vh, ph), (vh, pl), (vl, ph)], j == 0, j == 3,
                                  pt.sem if j == 3 else None)
            t = self.tmp.next()
            st[("O", h)] = (b, t, act.wait(mark, self.freed(t)).act(t.ap, b.ap, func=ACT.Square, sig="o_sq"))

        def sums_of(h):
            b, t, a = st[("O", h)]
            v, y, rc = self.small(4), self.small(4), self.small(4)
            pe.wait(a, self.freed(last))
            for c in range(4):
                mark = pe.mm(last.ap[:, c:c + 1], t.ap[:, 128 * c:128 * c + 128], self.ones[:, 0:1], True, True,
                             sig=t.sem if c == 3 else None)
            d = dve.do(lambda e: e.reciprocal(rc, st[("s", h)][0]), "o_var")
            d = dve.wait(mark, d).stt(v, last.ap[:, 0:4], 1.0 / 128, rc, ALU.mult, ALU.mult, sig=last.sem)
            d = dve.wait(d).tt(v, v, rc, ALU.mult, sig="o_var")
            d = dve.wait(d).ts(v, v, EPS, None, ALU.add, sig="o_var")
            d = self.newton(v, y, d)
            st[("y", h)] = (y, dve.wait(d).tt(y, y, rc, ALU.mult, sig="o_var"))

        def finish(h):
            b = st[("O", h)][0]
            y, d = st[("y", h)]
            pe.wait(d, self.freed(last))
            for c in range(4):
                mark = pe.mm(last.ap[:, 128 * c:128 * c + 128], y[:, c:c + 1].broadcast_to([P, P]), self.ident[:, :],
                             True, True, sig="pe_spread")
            t, r = self.tmp.next(), self.tmp.next()
            a = act.wait(mark, self.freed(r)).act(r.ap, last.ap, sig=last.sem)
            x = dve.wait(a, gsw, self.freed(t)).stt(t.ap, b.ap, gs, r.ap, ALU.mult, ALU.mult, sig=b.sem)
            hi, lo = KZ[:, 1024 * h:1024 * h + 512], KZ[:, 1024 * h + 512:1024 * h + 1024]
            a = act.wait(x, st[("sl", h)]).act(hi, t.ap, sig=r.sem)
            zw[h] = st["pool"] = self.pool.wait(a, st["pool"]).tt(lo, t.ap, hi.bitcast(F32), ALU.subtract, sig=t.sem)

        project(0)
        for h in range(8):
            scores(h, 0)
            if h:
                combine(h - 1, 3)
                turn(h - 1, 2)
            scores(h, 1)
            combine(h, 0)
            if h:
                turn(h - 1, 3)
            scores(h, 2)
            combine(h, 1)
            if h:
                values(h - 1)
            turn(h, 0)
            if h < 7:
                project(h + 1)
            if h:
                sums_of(h - 1)
            scores(h, 3)
            combine(h, 2)
            turn(h, 1)
            if h:
                finish(h - 1)
        combine(7, 3)
        turn(7, 2)

        def end():
            finish(7)
            self.tmp = slots

        self.out_proj("w_o_2", 8, lambda p, k: KZ[:, 1024 * k + 512 * p:1024 * k + 512 * p + 512], zw,
                      lambda: [self.freed(t) for t in extra], None,
                      {0: lambda: turn(7, 3), 1: lambda: values(7), 2: lambda: sums_of(7), 4: end})

    def build(self):
        sp, dve = self.sp, self.dve
        self.stream_start()
        n = COLS["g_post_a"]
        self.cold = sp.dma(self.cols[:, 0:n], self.ins["cols"][:, 0:n], "cols")
        xw = []
        for k in range(KD):
            xw.append(sp.dma(self.xt(k), self.ins["xT"][P * k:P * k + P, :], f"x{k}"))
            if k in (0, 2, 4):
                self.load_unit()
        self.cols_rest = sp.dma(self.cols[:, n:], self.ins["cols"][:, n:], "cols_rest")
        sp.dma(self.ident[:, :], self.ins["ident"][:, :], "consts")
        consts = sp.dma(self.masks[:, :], self.ins["masks"][:, :], "consts")
        dve.do(lambda e: e.memset(self.ones[:, :], 1.0), "ones")
        self.act.wait(self.cold)
        self.retention(xw)
        self.act.wait(self.cols_rest, consts)
        dve.wait(self.cols_rest, consts)
        self.latent(self.normed(1024, "g_post_a", 0))
        while len(self.order) % UNIT:
            self.order.append(None)
        self.mixer(self.normed(1024, "g_post_b", 0))
        self.ffn(0, self.normed(1024, "g_post_mix_2", 0))
        residual = self.ple(0)
        self.diff(residual)
        self.ffn(1, self.normed(1024, "g_post_mix_2", 8))
        scaled, added = self.ple(1)
        t = scaled(0)
        for k in range(KD):
            last, t = t, scaled(k + 1) if k + 1 < KD else None
            done = sp.wait(added(k, *last)).dma(self.out[P * k:P * k + P, :], self.xt(k), "out")
        sp.wait(done).do(lambda e: e.nop())
        assert -(-len(self.order) // UNIT) == self.NU, len(self.order)

    def emit(self):
        nc, ctx = self.nc, self.ctx
        sems = {n: ctx.enter_context(nc.semaphore("s_" + n)) for n in self.counts}
        block = ctx.enter_context(nc.Block())

        @block.sync
        def _(e):
            self.sp.issue(e, sems)

        @block.scalar
        def _(e):
            self.act.issue(e, sems)

        @block.vector
        def _(e):
            self.dve.issue(e, sems)

        @block.gpsimd
        def _(e):
            self.pool.issue(e, sems)

        @block.tensor
        def _(e):
            self.pe.issue(e, sems)


NUNITS = 311


def build_program(nc, ins, out):
    from contextlib import ExitStack

    with ExitStack() as ctx:
        p = Net(nc, ctx, ins, out)
        p.build()
        p.emit()
    return p.order


def shape_constants():
    f = np.float32
    heads = np.arange(8, dtype=np.float64)
    lg = np.log(1.0 - np.exp2(-5.0 - heads))
    k, q = np.arange(128)[:, None], np.arange(512)[None, :]
    ok = (k // 64) <= (q // 64)
    dec = np.exp(lg[:, None, None] * np.abs(q - k)[None]) * ok[None] * 128.0 ** -0.5
    out = {"decay": dec.reshape(8 * 128, 512).astype(f)}
    pos = np.arange(512, dtype=f)

    def angles(half):
        inv = (f(10000.0) ** (-np.arange(half, dtype=f) / f(half))).astype(f)
        return (pos[:, None] * inv[None, :]).astype(f).astype(np.float64).T

    for name, half in (("rope_a", 64), ("rope_b", 32)):
        a = angles(half)
        i = np.arange(128) % half
        c, s = np.cos(a)[i], np.sin(a)[i]
        s = np.where(np.arange(128)[:, None] < 64, s, -s)
        out[name] = np.concatenate([c, s], axis=1).astype(f)
    out["ident"] = np.eye(128, dtype=f)
    qq, kk = np.arange(128)[:, None], np.arange(128)[None, :]
    out["mask"] = np.where(kk // 64 <= qq // 64, 0.0, NEG).astype(f)
    par = (np.arange(128) // 32) % 2
    out["masks"] = np.stack([par == 0, par == 1], axis=1).astype(f)
    dist = 511 - np.arange(TW)
    d = np.maximum(dist, 1).astype(f)
    large = 16 + (np.log(d / f(16)).astype(f) / f(math.log(128 / 16)) * f(16)).astype(np.int32)
    bucket = np.where(dist < 16, dist, np.minimum(large, 31))
    oh = np.zeros((33, TW), f)
    for e in range(TW):
        if dist[e] >= 0:
            oh[bucket[e], e] = 1.0
        else:
            oh[32, e] = 1.0
    out["onehot"] = oh
    return out


def lay_out(inputs, order):
    f = np.float32
    a = {n: np.asarray(v) for n, v in inputs.items()}
    w = {"w_in_a": a["w_in_a"][0], "w_out_a": a["w_out_a"][0], "w_kv_a": a["w_kv_a"], "w_uk": a["w_uk"],
         "w_uv": a["w_uv"], "w_in_b": a["w_in_b"][0], "w_uq": a["w_uq"][0], "w_out_b": a["w_out_b"][0],
         "w_sc_in_2": a["w_sc_in_2"][0], "w_sc_out_2": a["w_sc_out_2"][0], "w_kv_2": a["w_kv_2"],
         "w_q_2": a["w_q_2"][0], "w_o_2": a["w_o_2"][0]}
    for n in ("w_ffn_up_2", "w_ffn_down_2", "w_ple_gate_2", "w_ple_proj_2"):
        for L in range(2):
            w[f"{n}_{L}"] = a[n][L]
    ws = np.zeros((NUNITS, 128, UNIT, 128), f)
    for i, block in enumerate(order):
        if block is None:
            continue
        name, k, cols = block
        m = w[name][128 * k:128 * k + 128]
        ws[i // UNIT, :, i % UNIT, :] = m[:, 128 * cols:128 * cols + 128] if isinstance(cols, int) else m[:, cols]
    out = {"ws": ws.reshape(-1, 128 * UNIT)}
    cols = np.zeros((128, NCOL), f)
    for n, at in COLS.items():
        v = a[n].reshape(-1, 128).T
        cols[:, at:at + v.shape[1]] = v
    out["cols"] = cols
    out["xT"] = np.ascontiguousarray(a["x"][0].T)
    out["pT"] = np.ascontiguousarray(a["p_2"][:, 0].transpose(0, 2, 1).reshape(512, 512))
    rb = np.full((33, 8), NEG, f)
    rb[0:32] = a["rel_bias_2"]
    out["rb"] = rb
    out["lam"] = np.ascontiguousarray(a["diff_lambda_2"].reshape(1, 256))
    return out


def kernel(**inputs):
    import concourse.bacc as _bacc
    from concourse.bass_utils import run_bass_kernel_spmd as _run

    nc = _bacc.Bacc("TRN2", target_bir_lowering=False, num_devices=1, dynamic_dma_scratch_size=256)
    consts = shape_constants()
    shapes = {n: v.shape for n, v in consts.items()}
    shapes.update(ws=(NUNITS * 128, 128 * UNIT), cols=(128, NCOL), xT=(1024, 512), pT=(512, 512), rb=(33, 8),
                  lam=(1, 256))
    ins = {n: nc.dram_tensor("in_" + n, s, F32, kind="ExternalInput").ap() for n, s in shapes.items()}
    ins["scr"] = nc.dram_tensor("scr", (8, 128 * (TW + 1)), F32).ap()
    out = nc.dram_tensor("out_0_dram", (1024, 512), F32, kind="ExternalOutput").ap()
    order = build_program(nc, ins, out)
    arrays = lay_out(inputs, order)
    arrays.update(consts)
    r = _run(nc, [{"in_" + n: v for n, v in arrays.items()}], core_ids=[0])
    got = r.results[0]["out_0_dram"]
    return np.ascontiguousarray(got.T).reshape(1, 512, 1024)
```
